# Optimizing a Trainium2 kernel written in Bass

```python
import math
import jax, jax.numpy as jnp
from jax import lax
import numpy as np

D_MODEL = 1024
BATCH = 1
SEQ = 2048
DEPTH = 1
DEC_BATCH = 8
DEC_SEQ = 1
PAST_LEN = 8192
PAGE_SIZE = 128

D_MIX = D_MODEL
N_ATT_HEADS = 8
ATT_HEAD_DIM = 64
N_KV_HEADS = 2
D_ATT = N_ATT_HEADS * ATT_HEAD_DIM
KV_DIM = N_KV_HEADS * ATT_HEAD_DIM
N_IDX_HEADS = 16
IDX_DIM = 64
TOPK_MAX = 256
N_GDN_HEADS = 4
GDN_HEAD_DIM = 128
D_GDN = N_GDN_HEADS * GDN_HEAD_DIM
CONV_W = 4
GDN_CHUNK = 64
N_BUCKETS = 32
MAX_DISTANCE = 128
Q_BLOCK = 128
RMS_EPS = 1e-6
NEG_BIG = -1e30
PROJ_SIZES = (D_ATT, KV_DIM, KV_DIM, D_ATT, N_IDX_HEADS * IDX_DIM, IDX_DIM, N_IDX_HEADS,
              3 * D_GDN, D_GDN, N_GDN_HEADS, N_GDN_HEADS)
D_PROJ = sum(PROJ_SIZES)

kernel_name = 'hymba_dsa_gdn_decode_step'

def _rmsnorm(x, g):
    xf = x.astype(jnp.float32)
    y = xf * lax.rsqrt(jnp.mean(xf * xf, axis=-1, keepdims=True) + RMS_EPS)
    return (y * g.astype(jnp.float32)).astype(x.dtype)

def _l2norm(x):
    return x * lax.rsqrt(jnp.sum(x * x, axis=-1, keepdims=True) + 1e-6)

def _rel_bucket(dist):
    n = jnp.maximum(dist, 0)
    max_exact = N_BUCKETS // 2
    nf = jnp.maximum(n, 1).astype(jnp.float32)
    large = max_exact + (jnp.log(nf / max_exact) / math.log(MAX_DISTANCE / max_exact)
                         * (N_BUCKETS - max_exact)).astype(jnp.int32)
    large = jnp.minimum(large, N_BUCKETS - 1)
    return jnp.where(n < max_exact, n, large)

def _mixer_inputs(x, norm_g, w_in):
    B, T, _ = x.shape
    h = _rmsnorm(x, norm_g)
    splits = np.cumsum(PROJ_SIZES)[:-1].tolist()
    q, k, v, z_a, qi, ki, wi, qkv, z_g, a_g, b_g = jnp.split(h @ w_in, splits, axis=-1)
    return (q.reshape(B, T, N_ATT_HEADS, ATT_HEAD_DIM),
            k.reshape(B, T, N_KV_HEADS, ATT_HEAD_DIM),
            v.reshape(B, T, N_KV_HEADS, ATT_HEAD_DIM),
            z_a, qi.reshape(B, T, N_IDX_HEADS, IDX_DIM), ki, wi, qkv, z_g, a_g, b_g)

def _indexer_scores(qi, wi, ki):
    s = jnp.einsum('...thd,...sd->...ths', qi.astype(jnp.float32), ki.astype(jnp.float32)) * (IDX_DIM ** -0.5)
    return jnp.einsum('...ths,...th->...ts', jax.nn.relu(s), wi.astype(jnp.float32)) * (N_IDX_HEADS ** -0.5)

def _sparse_attend(q, k_sel, v_sel, valid, bias):
    *lead, T, H, Dh = q.shape
    K = k_sel.shape[-3]
    G = H // N_KV_HEADS
    qg = q.reshape(*lead, T, N_KV_HEADS, G, Dh).astype(jnp.float32)
    logits = jnp.einsum('...tgrd,...tkgd->...tgrk', qg, k_sel.astype(jnp.float32)) * (Dh ** -0.5)
    b = jnp.moveaxis(bias.astype(jnp.float32).reshape(*lead, T, K, N_KV_HEADS, G), -3, -1)
    logits = jnp.where(valid[..., :, None, None, :], logits + b, NEG_BIG)
    p = jax.nn.softmax(logits, axis=-1)
    o = jnp.einsum('...tgrk,...tkgd->...tgrd', p, v_sel.astype(jnp.float32))
    return o.reshape(*lead, T, H * Dh)

def _dsa_prompt(q, k, v, qi, ki, wi, rel_table):
    B, S = q.shape[:2]
    topk = min(TOPK_MAX, S // 4)
    n_blocks = S // Q_BLOCK
    kpos = jnp.arange(S)

    def per_seq(args):
        q1, k1, v1, qi1, ki1, wi1 = args

        def per_block(bi):
            t0 = bi * Q_BLOCK
            qb = lax.dynamic_slice_in_dim(q1, t0, Q_BLOCK, 0)
            qib = lax.dynamic_slice_in_dim(qi1, t0, Q_BLOCK, 0)
            wib = lax.dynamic_slice_in_dim(wi1, t0, Q_BLOCK, 0)
            qpos = t0 + jnp.arange(Q_BLOCK)
            sc = _indexer_scores(qib, wib, ki1)
            sc = jnp.where(kpos[None, :] <= qpos[:, None], sc, NEG_BIG)
            _, sel = lax.top_k(sc, topk)
            valid = sel <= qpos[:, None]
            bias = rel_table[_rel_bucket(qpos[:, None] - sel)]
            return _sparse_attend(qb, k1[sel], v1[sel], valid, bias)

        return lax.map(per_block, jnp.arange(n_blocks)).reshape(S, D_ATT)

    return lax.map(per_seq, (q, k, v, qi, ki, wi))

def _dsa_sample(q, k_new, v_new, qi, ki_new, wi, cache_k, cache_v, cache_kidx, layer, page_table, rel_table):
    Bd, T = q.shape[:2]
    n_pages = page_table.shape[1]
    P = n_pages * PAGE_SIZE
    L = P + T
    topk = min(TOPK_MAX, L // 4)
    ki_past = cache_kidx[layer, page_table].reshape(Bd, P, IDX_DIM)
    ki_all = jnp.concatenate([ki_past.astype(ki_new.dtype), ki_new], axis=1)
    qpos = P + jnp.arange(T)
    kpos = jnp.arange(L)
    sc = _indexer_scores(qi, wi, ki_all)
    sc = jnp.where(kpos[None, None, :] <= qpos[None, :, None], sc, NEG_BIG)
    _, sel = lax.top_k(sc, topk)
    valid = sel <= qpos[None, :, None]
    in_past = (sel < P)[..., None, None]
    sp = jnp.minimum(sel, P - 1)
    bidx = jnp.arange(Bd)[:, None, None]
    phys = page_table[bidx, sp // PAGE_SIZE]
    off = sp % PAGE_SIZE
    sn = jnp.clip(sel - P, 0, T - 1)
    k_sel = jnp.where(in_past, cache_k[layer, phys, off].astype(k_new.dtype), k_new[bidx, sn])
    v_sel = jnp.where(in_past, cache_v[layer, phys, off].astype(v_new.dtype), v_new[bidx, sn])
    bias = rel_table[_rel_bucket(qpos[None, :, None] - sel)]
    return _sparse_attend(q, k_sel, v_sel, valid, bias)

def _causal_conv(x_ext, w):
    T = x_ext.shape[1] - (CONV_W - 1)
    out = x_ext[:, 0:T] * w[0]
    for j in range(1, CONV_W):
        out = out + x_ext[:, j:j + T] * w[j]
    return jax.nn.silu(out)

def _gdn_features(qkv_c, a_g, b_g, a_log, dt_bias):
    B, T, _ = qkv_c.shape
    q, k, v = jnp.split(qkv_c.astype(jnp.float32), 3, axis=-1)
    q = _l2norm(q.reshape(B, T, N_GDN_HEADS, GDN_HEAD_DIM)) * (GDN_HEAD_DIM ** -0.5)
    k = _l2norm(k.reshape(B, T, N_GDN_HEADS, GDN_HEAD_DIM))
    v = v.reshape(B, T, N_GDN_HEADS, GDN_HEAD_DIM)
    g = -jnp.exp(a_log.astype(jnp.float32)) * jax.nn.softplus(a_g.astype(jnp.float32) + dt_bias.astype(jnp.float32))
    beta = jax.nn.sigmoid(b_g.astype(jnp.float32))
    return q, k, v, g, beta

def _gdn_chunked(q, k, v, g, beta):
    B, T, H, Dk = q.shape
    Dv = v.shape[-1]
    C = GDN_CHUNK
    N = T // C

    def chunkify(x):
        return x.reshape(B, N, C, H, -1).transpose(0, 3, 1, 2, 4)

    qc, kc, vc = chunkify(q), chunkify(k), chunkify(v)
    gc = g.reshape(B, N, C, H).transpose(0, 3, 1, 2)
    bc = beta.reshape(B, N, C, H).transpose(0, 3, 1, 2)
    gcum = jnp.cumsum(gc, axis=-1)
    tril = jnp.tril(jnp.ones((C, C), dtype=bool))
    strict = jnp.tril(jnp.ones((C, C), dtype=bool), -1)
    diff = gcum[..., :, None] - gcum[..., None, :]
    decay = jnp.where(tril, jnp.exp(jnp.where(tril, diff, 0.0)), 0.0)
    kb = kc * bc[..., None]
    vb = vc * bc[..., None]
    a_mat = jnp.where(strict, jnp.einsum('bhncd,bhnsd->bhncs', kb, kc) * decay, 0.0)
    u = lax.linalg.triangular_solve(a_mat, vb, left_side=True, lower=True, unit_diagonal=True)
    w = lax.linalg.triangular_solve(a_mat, kb * jnp.exp(gcum)[..., None], left_side=True, lower=True, unit_diagonal=True)
    attn_qk = jnp.einsum('bhncd,bhnsd->bhncs', qc, kc) * decay
    q_dec = qc * jnp.exp(gcum)[..., None]
    k_dec = kc * jnp.exp(gcum[..., -1:] - gcum)[..., None]
    chunk_dec = jnp.exp(gcum[..., -1])

    def step(S, xs):
        q_d, k_d, u_i, w_i, a_i, dec = xs
        v_new = u_i - jnp.einsum('bhcd,bhde->bhce', w_i, S)
        o = jnp.einsum('bhcd,bhde->bhce', q_d, S) + jnp.einsum('bhcs,bhse->bhce', a_i, v_new)
        S = S * dec[..., None, None] + jnp.einsum('bhcd,bhce->bhde', k_d, v_new)
        return S, o

    xs = tuple(jnp.moveaxis(t, 2, 0) for t in (q_dec, k_dec, u, w, attn_qk, chunk_dec))
    S0 = jnp.zeros((B, H, Dk, Dv), jnp.float32)
    S_fin, o = lax.scan(step, S0, xs)
    o = o.transpose(1, 0, 3, 2, 4).reshape(B, T, H, Dv)
    return o, S_fin

def _gdn_recurrent(q, k, v, g, beta, S0):
    def step(S, xs):
        q_t, k_t, v_t, g_t, b_t = xs
        S = S * jnp.exp(g_t)[..., None, None]
        kv = jnp.einsum('bhd,bhde->bhe', k_t, S)
        delta = (v_t - kv) * b_t[..., None]
        S = S + jnp.einsum('bhd,bhe->bhde', k_t, delta)
        return S, jnp.einsum('bhd,bhde->bhe', q_t, S)

    xs = tuple(jnp.moveaxis(t, 1, 0) for t in (q, k, v, g, beta))
    S_fin, o = lax.scan(step, S0.astype(jnp.float32), xs)
    return jnp.moveaxis(o, 0, 1), S_fin

def _merge(x, att_o, z_a, gdn_o, z_g, gdn_norm_g, w_out):
    B, T = x.shape[:2]
    att = att_o * jax.nn.silu(z_a.astype(jnp.float32))
    gdn = _rmsnorm(gdn_o, gdn_norm_g).reshape(B, T, D_GDN) * jax.nn.silu(z_g.astype(jnp.float32))
    mixed = jnp.concatenate([att, gdn], axis=-1).astype(x.dtype)
    return x + mixed @ w_out

def setup_inputs(seed: int = 0) -> dict:
    key = jax.random.key(seed)
    ks = jax.random.split(key, 20)
    f32 = jnp.float32
    n_pages = PAST_LEN // PAGE_SIZE
    n_pool = (DEC_BATCH * n_pages * 5) // 4
    x_prompt = jax.random.normal(ks[0], (BATCH, SEQ, D_MODEL), f32)
    x_sample = jax.random.normal(ks[1], (DEC_BATCH, DEC_SEQ, D_MODEL), f32)
    cache_k = jax.random.normal(ks[2], (DEPTH, n_pool, PAGE_SIZE, N_KV_HEADS, ATT_HEAD_DIM), f32)
    cache_v = jax.random.normal(ks[3], (DEPTH, n_pool, PAGE_SIZE, N_KV_HEADS, ATT_HEAD_DIM), f32)
    cache_kidx = jax.random.normal(ks[4], (DEPTH, n_pool, PAGE_SIZE, IDX_DIM), f32)
    state_ssm = 0.1 * jax.random.normal(ks[5], (DEPTH, DEC_BATCH, N_GDN_HEADS, GDN_HEAD_DIM, GDN_HEAD_DIM), f32)
    state_conv = jax.random.normal(ks[6], (DEPTH, DEC_BATCH, CONV_W - 1, 3 * D_GDN), f32)
    page_table = jax.random.permutation(ks[7], n_pool)[:DEC_BATCH * n_pages].reshape(DEC_BATCH, n_pages).astype(jnp.int32)
    norm_in = 1.0 + 0.01 * jax.random.normal(ks[8], (DEPTH, D_MODEL), f32)
    w_in = jax.random.normal(ks[9], (DEPTH, D_MODEL, D_PROJ), f32) * (D_MODEL ** -0.5)
    conv_w = jax.random.normal(ks[10], (DEPTH, CONV_W, 3 * D_GDN), f32) * (CONV_W ** -0.5)
    a_log = jnp.log(jax.random.uniform(ks[11], (DEPTH, N_GDN_HEADS), f32, 1.0, 16.0))
    dt = jnp.exp(jax.random.uniform(ks[12], (DEPTH, N_GDN_HEADS), f32, math.log(1e-3), math.log(1e-1)))
    dt_bias = dt + jnp.log(-jnp.expm1(-dt))
    gdn_norm = 1.0 + 0.01 * jax.random.normal(ks[13], (DEPTH, GDN_HEAD_DIM), f32)
    w_out = jax.random.normal(ks[14], (DEPTH, D_MIX, D_MODEL), f32) * (D_MIX ** -0.5)
    rel_table = 0.5 * jax.random.normal(ks[15], (N_BUCKETS, N_ATT_HEADS), f32)
    norm_final = 1.0 + 0.01 * jax.random.normal(ks[16], (D_MODEL,), f32)
    return {'x_prompt': x_prompt, 'x_sample': x_sample, 'cache_k': cache_k, 'cache_v': cache_v,
            'cache_kidx': cache_kidx, 'state_ssm': state_ssm, 'state_conv': state_conv,
            'page_table': page_table, 'norm_in': norm_in, 'w_in': w_in, 'conv_w': conv_w,
            'a_log': a_log, 'dt_bias': dt_bias, 'gdn_norm': gdn_norm, 'w_out': w_out,
            'rel_table': rel_table, 'norm_final': norm_final}

def reference(x_prompt, x_sample, cache_k, cache_v, cache_kidx, state_ssm, state_conv, page_table,
              norm_in, w_in, conv_w, a_log, dt_bias, gdn_norm, w_out, rel_table, norm_final):
    hp, hs = x_prompt, x_sample
    kp_l, vp_l, kip_l, sp_l, cp_l = [], [], [], [], []
    ks_l, vs_l, kis_l, ss_l, cs_l = [], [], [], [], []
    for l in range(DEPTH):
        q, k, v, z_a, qi, ki, wi, qkv, z_g, a_g, b_g = _mixer_inputs(hp, norm_in[l], w_in[l])
        att = _dsa_prompt(q, k, v, qi, ki, wi, rel_table)
        qkv_c = _causal_conv(jnp.pad(qkv, ((0, 0), (CONV_W - 1, 0), (0, 0))), conv_w[l])
        gq, gk, gv, g, beta = _gdn_features(qkv_c, a_g, b_g, a_log[l], dt_bias[l])
        gdn, s_fin = _gdn_chunked(gq, gk, gv, g, beta)
        hp = _merge(hp, att, z_a, gdn, z_g, gdn_norm[l], w_out[l])
        kp_l.append(k)
        vp_l.append(v)
        kip_l.append(ki)
        sp_l.append(s_fin.astype(x_prompt.dtype))
        cp_l.append(qkv[:, -(CONV_W - 1):])
        q, k, v, z_a, qi, ki, wi, qkv, z_g, a_g, b_g = _mixer_inputs(hs, norm_in[l], w_in[l])
        att = _dsa_sample(q, k, v, qi, ki, wi, cache_k, cache_v, cache_kidx, l, page_table, rel_table)
        conv_ext = jnp.concatenate([state_conv[l].astype(qkv.dtype), qkv], axis=1)
        qkv_c = _causal_conv(conv_ext, conv_w[l])
        gq, gk, gv, g, beta = _gdn_features(qkv_c, a_g, b_g, a_log[l], dt_bias[l])
        gdn, s_new = _gdn_recurrent(gq, gk, gv, g, beta, state_ssm[l])
        hs = _merge(hs, att, z_a, gdn, z_g, gdn_norm[l], w_out[l])
        ks_l.append(k)
        vs_l.append(v)
        kis_l.append(ki)
        ss_l.append(s_new.astype(state_ssm.dtype))
        cs_l.append(conv_ext[:, -(CONV_W - 1):])
    y_prompt = _rmsnorm(hp, norm_final)
    y_sample = _rmsnorm(hs, norm_final)
    return (y_prompt, y_sample,
            jnp.stack(kp_l), jnp.stack(vp_l), jnp.stack(kip_l), jnp.stack(sp_l), jnp.stack(cp_l),
            jnp.stack(ks_l), jnp.stack(vs_l), jnp.stack(kis_l), jnp.stack(ss_l), jnp.stack(cs_l))


_drawn_inputs = setup_inputs


def setup_inputs(seed=0):
    import zlib

    import numpy as np

    out = dict(_drawn_inputs(seed))
    spreads = {}
    factors = {'norm_in': 3.896, 'gdn_norm': 8.0, 'rel_table': 3.991, 'norm_final': 5.718}
    for name, (base, spread) in spreads.items():
        noise = np.random.default_rng([zlib.crc32(name.encode()), seed]).standard_normal(out[name].shape)
        drawn = base * np.exp(spread * noise) if base else spread * noise
        out[name] = __import__('jax').numpy.asarray(drawn.astype(out[name].dtype))
    for name, factor in factors.items():
        out[name] = (out[name] * factor).astype(out[name].dtype)
    return out
```

```python
from contextlib import ExitStack

import numpy as np
import concourse.bass as bass
from concourse import mybir

F32 = mybir.dt.float32
I32 = mybir.dt.int32
U32 = mybir.dt.uint32
ALU = mybir.AluOpType
ACT = mybir.ActivationFunctionType
AX = mybir.AxisListType

P = 128
D_MODEL = 1024
KB = D_MODEL // P
SEQ = 2048
NT = SEQ // P
NB = 8
HEADS, DH = 8, 64
KV_HEADS = 2
IDX_HEADS = 16
G_HEADS, GD = 4, 128
CONV_W = 4
PAGE = 128
N_PAGES = 64
PAST = PAGE * N_PAGES
TOPK = 256
N_BUCKETS = 32
EPS = 1e-6
NEG = -1e30
C_Q, C_K, C_V, C_ZA, C_QI, C_KI, C_WI, C_QKV, C_ZG, C_A, C_B = (
    0, 512, 640, 768, 1280, 2304, 2368, 2384, 3920, 4432, 4436)
T_K, T_V, T_KI, T_WI, T_A, T_B, T_SMALL = 0, 128, 256, 320, 336, 340, 344
T_ALL = T_SMALL + 1024
F_Q, F_QI, F_QKV, F_ALL = 0, 512, 1536, 3072
NQB, NQIB, NGB = 4, 8, 12
LAST = CONV_W - 1
SMALL_ROWS = NB + LAST
BUCKET_START = [0, 1, 2, 3, 4, 5, 6, 7, 8, 9, 10, 11, 12, 13, 14, 15, 16, 19, 21, 24, 27, 31, 35, 40, 46,
                52, 59, 67, 77, 87, 99, 113]


class Scope:

    def __init__(self, nc, ctx):
        self.nc, self.ctx, self.sems = nc, ctx, []
        ctx.callback(self.clear)

    def sb(self, name, shape, dt=F32):
        return self.ctx.enter_context(self.nc.sbuf_tensor(name, shape, dt))

    def ps(self, name, shape, dt=F32):
        return self.ctx.enter_context(self.nc.psum_tensor(name, shape, dt))

    def sem(self, name):
        self.sems.append(self.nc.alloc_semaphore(name=name))
        return self.sems[-1]

    def clear(self):
        if self.sems:
            self.nc.clear_and_free_semaphores(self.sems)
            self.nc.all_engine_barrier()


def constants(nc, keep):
    with ExitStack() as ctx:
        s = Scope(nc, ctx)
        filled, done = s.sem("const_filled"), s.sem("const_done")
        block = ctx.enter_context(nc.Block())

        @block.gpsimd
        def _(pool):
            pool.memset(keep["ident"][:, :], 0.0).then_inc(filled, 1)
            pool.memset(keep["upper"][:, :], 1.0).then_inc(filled, 1)
            pool.memset(keep["ones"][:, :], 1.0).then_inc(filled, 1)
            pool.memset(keep["minus_half"][:, :], -0.5).then_inc(filled, 1)
            pool.wait_ge(filled, 4)
            pool.affine_select(out=keep["ident"][:, :], in_=keep["ident"][:, :], compare_op=ALU.not_equal,
                               fill=1.0, base=0, pattern=[[-1, P]], channel_multiplier=1).then_inc(done, 1)
            pool.affine_select(out=keep["upper"][:, :], in_=keep["upper"][:, :], compare_op=ALU.is_ge,
                               fill=0.0, base=0, pattern=[[1, P]], channel_multiplier=-1).then_inc(done, 1)
            pool.wait_ge(done, 2)


def project_tokens(nc, d, keep, hT, h_small):
    with ExitStack() as ctx:
        s = Scope(nc, ctx)
        w_tok = s.sb("w_tok", [P, KB, T_ALL])
        norm_w = s.sb("norm_w", [P, KB])
        x_in = s.sb("x_in", [P, 2, D_MODEL])
        x_n = s.sb("x_n", [P, 2, D_MODEL])
        h_tile = s.sb("h_tile", [P, 2, KB, P])
        gate = s.sb("gate", [P, 2, 1024])
        ssum = s.sb("ssum", [P, 2])
        rinv = s.sb("rinv", [P, 2])
        ps_t = s.ps("ps_t", [P, KB, P])
        ps_o = [s.ps(f"ps_o{i}", [P, 512]) for i in range(6)]
        x_loaded = [s.sem(f"x_loaded{u}") for u in range(2)]
        gate_stored = [s.sem(f"gate_stored{u}") for u in range(2)]
        names = ("w_loaded", "x_free", "ss_ready", "mean_ready", "rinv_ready", "xn_ready", "xn_free",
                 "xT_ready", "hT_ready", "hT_free", "h_all", "tok_ready", "tok_free",
                 "kept_stored", "h_small_ready")
        (w_loaded, x_free, ss_ready, mean_ready, rinv_ready, xn_ready, xn_free, xT_ready, hT_ready,
         hT_free, h_all, tok_ready, tok_free, kept_stored, h_small_ready) = (
            s.sem(n) for n in names)
        block = ctx.enter_context(nc.Block())
        CH = [(0, T_SMALL), (T_SMALL, 512), (T_SMALL + 512, 512)]

        @block.sync
        def _(sp):
            def load(t, u, rows):
                sp.wait_ge(x_free, t + 1)
                src = d["x_sample"] if rows == NB else d["x_prompt"][bass.ds(t * P, P), :]
                sp.dma_start(x_in[0:rows, u, :], src).then_inc(x_loaded[u], 16)

            load(0, 0, P)
            sp.dma_start(norm_w[:, :], d["norm_in"].rearrange("(b p) -> p b", p=P)).then_inc(w_loaded, 16)
            w = d["w_in"].rearrange("(b p) n -> p b n", p=P)
            for dst, src, n in ((T_K, C_K, 256), (T_KI, C_KI, 80), (T_A, C_A, 8), (T_SMALL, C_ZA, 512),
                                (T_SMALL + 512, C_ZG, 512)):
                sp.dma_start(w_tok[:, :, dst:dst + n], w[:, :, src:src + n]).then_inc(w_loaded, 16)
            load(1, 1, P)
            with sp.Fori(1, NT // 2) as j:
                for u in range(2):
                    load(2 * j + u, u, P)
            load(NT, 0, NB)

        @block.vector
        def _(dve):
            dve.sem_inc(x_free, 2)
            dve.wait_ge(w_loaded, 96)

            def tile(t, j, u, rows):
                dve.wait_ge(x_loaded[u], 16 * j + 16)
                dve.wait_ge(xn_free, t + 1)
                dve.tensor_tensor(x_n[0:rows, u, :], x_in[0:rows, u, :], x_in[0:rows, u, :], ALU.mult).then_inc(
                    ss_ready, 1)
                dve.wait_ge(ss_ready, 2 * t + 1)
                dve.tensor_reduce(ssum[0:rows, u:u + 1], x_n[0:rows, u, :], AX.X, ALU.add).then_inc(ss_ready, 1)
                dve.wait_ge(ss_ready, 2 * t + 2)
                dve.tensor_scalar(ssum[0:rows, u:u + 1], ssum[0:rows, u:u + 1], 1.0 / D_MODEL, EPS,
                                  ALU.mult, ALU.add).then_inc(mean_ready, 1)
                dve.wait_ge(rinv_ready, t + 1)
                dve.tensor_scalar(x_n[0:rows, u, :], x_in[0:rows, u, :], rinv[0:rows, u:u + 1], None,
                                  ALU.mult).then_inc(xn_ready, 1)
                dve.wait_ge(xn_ready, t + 1)
                dve.sem_inc(x_free, 1)
                dve.wait_ge(xT_ready, t + 1)
                dve.wait_ge(hT_free, t + 1)
                dve.tensor_tensor(h_tile[:, u, :, 0:rows], ps_t[:, :, 0:rows],
                                  norm_w[:, :].unsqueeze(2).broadcast_to([P, KB, rows]),
                                  ALU.mult).then_inc(hT_ready, 1)
                dve.wait_ge(hT_ready, t + 1)
                if rows == P:
                    dve.tensor_copy(hT[:, :, bass.ds(t * P, P)], h_tile[:, u, :, :]).then_inc(h_all, 1)
                else:
                    dve.tensor_copy(h_small[:, :, 0:NB], h_tile[:, u, :, 0:rows]).then_inc(h_all, 1)

            with dve.Fori(0, NT // 2) as j:
                for u in range(2):
                    tile(2 * j + u, j, u, P)
            tile(NT, NT // 2, 0, NB)
            dve.wait_ge(h_all, NT)
            dve.tensor_copy(h_small[:, :, NB:], hT[:, :, SEQ - LAST:SEQ]).then_inc(h_small_ready, 1)

        @block.gpsimd
        def _(pool):
            def tile(t, u, rows):
                pool.wait_ge(mean_ready, t + 1)
                pool.tensor_tensor(rinv[0:rows, u:u + 1], ssum[0:rows, u:u + 1], keep["minus_half"][0:rows, 0:1],
                                   ALU.pow).then_inc(rinv_ready, 1)

            with pool.Fori(0, NT // 2) as j:
                for u in range(2):
                    tile(2 * j + u, u, P)
            tile(NT, 0, NB)

        @block.tensor
        def _(pe):
            pe.sem_inc(xn_free, 2)
            pe.sem_inc(hT_free, 2)

            def transposes(t, u, rows, first=False):
                pe.wait_ge(xn_ready, t + 1)
                if not first:
                    pe.wait_ge(hT_ready, t)
                for b in range(KB):
                    last = pe.transpose(ps_t[:, b, 0:rows], x_n[0:rows, u, b * P:(b + 1) * P],
                                        keep["ident"][0:rows, 0:rows])
                last.then_inc(xT_ready, 1)
                pe.wait_ge(xT_ready, t + 1)
                pe.sem_inc(xn_free, 1)

            def products(t, u, rows):
                pe.wait_ge(hT_ready, t + 1)
                for c, (c0, n) in enumerate(CH):
                    pe.wait_ge(tok_free, 3 * t + c + 1)
                    for b in range(KB):
                        last = pe.matmul(ps_o[3 * u + c][0:rows, 0:n], h_tile[:, u, b, 0:rows],
                                         w_tok[:, b, c0:c0 + n], start=(b == 0), stop=(b == KB - 1))
                    last.then_inc(tok_ready, 1)
                pe.wait_ge(tok_ready, 3 * t + 3)
                pe.sem_inc(hT_free, 1)

            transposes(0, 0, P, first=True)
            pe.wait_ge(w_loaded, 96)
            with pe.Fori(0, NT // 2 - 1) as j:
                for u in range(2):
                    transposes(2 * j + u + 1, 1 - u, P)
                    products(2 * j + u, u, P)
            transposes(NT - 1, 1, P)
            products(NT - 2, 0, P)
            transposes(NT, 0, NB)
            products(NT - 1, 1, P)
            products(NT, 0, NB)

        @block.scalar
        def _(act):
            act.sem_inc(tok_free, 6)

            def tile(t, j, u, rows, first=False):
                act.wait_ge(tok_ready, 3 * t + 1)
                dst = keep["samp"][:, :] if rows == NB else keep["tok"][:, bass.ds(t, 1), :].squeeze(1) \
                    if not isinstance(t, int) else keep["tok"][:, t, :]
                act.activation(dst, ps_o[3 * u][0:rows, 0:T_SMALL], ACT.Copy).then_inc(tok_free, 1)
                if not first:
                    act.wait_ge(gate_stored[u], 16 * j)
                for c in (1, 2):
                    act.wait_ge(tok_ready, 3 * t + 1 + c)
                    out = keep["samp_gate"][:, 512 * (c - 1):512 * c] if rows == NB else \
                        gate[:, u, 512 * (c - 1):512 * c]
                    act.activation(out, ps_o[3 * u + c][0:rows, :], ACT.Silu).then_inc(tok_free, 1)
                if rows == P:
                    act.wait_ge(tok_free, 6 + 3 * t + 3)
                    act.dma_start(d["gates"][bass.ds(t * P, P), :], gate[:, u, :]).then_inc(gate_stored[u], 16)

            tile(0, 0, 0, P, first=True)
            tile(1, 0, 1, P, first=True)
            with act.Fori(1, NT // 2) as j:
                for u in range(2):
                    tile(2 * j + u, j, u, P)
            tile(NT, NT // 2, 0, NB)
            act.wait_ge(tok_free, 6 + 3 * NT + 3)
            for name, c0, n in (("k_prompt", T_K, 128), ("v_prompt", T_V, 128), ("kidx_prompt", T_KI, 64)):
                act.dma_start(d[name].rearrange("(t p) f -> p t f", p=P),
                              keep["tok"][:, :, c0:c0 + n]).then_inc(kept_stored, 16)
            for name, c0, n in (("k_sample", T_K, 128), ("v_sample", T_V, 128), ("kidx_sample", T_KI, 64)):
                act.dma_start(d[name], keep["samp"][:, c0:c0 + n]).then_inc(kept_stored, 16)
            for u in range(2):
                act.wait_ge(gate_stored[u], 8 * NT)
            act.wait_ge(kept_stored, 16 * 6)


def transpose_keys(nc, keep):
    with ExitStack() as ctx:
        s = Scope(nc, ctx)
        ps = [s.ps(f"ps_k{i}", [DH, 512]) for i in range(3)]
        turned, copied = s.sem("key_turned"), s.sem("key_copied")
        block = ctx.enter_context(nc.Block())
        jobs = [(c0, n) for n in range(4) for c0 in (T_K, T_K + DH, T_KI)]

        @block.tensor
        def _(pe):
            for m, (c0, n) in enumerate(jobs):
                if m >= 3:
                    pe.wait_ge(copied, m - 2)
                for i in range(4):
                    last = pe.transpose(ps[m % 3][:, i * P:(i + 1) * P], keep["tok"][:, 4 * n + i, c0:c0 + DH],
                                        keep["ident"][:, :])
                last.then_inc(turned, 1)

        @block.scalar
        def _(act):
            for m, (c0, n) in enumerate(jobs):
                act.wait_ge(turned, m + 1)
                dst = keep["kidxT"][:, n * 512:(n + 1) * 512] if c0 == T_KI else \
                    keep["keyT"][:, (c0 - T_K) // DH, n * 512:(n + 1) * 512]
                act.activation(dst, ps[m % 3][:, :], ACT.Copy).then_inc(copied, 1)


def project_features(nc, d, keep, hT, h_small):
    with ExitStack() as ctx:
        s = Scope(nc, ctx)
        w_blk = s.sb("w_blk", [P, 2, KB, P])
        out = s.sb("out_stage", [P, 2, SEQ])
        raw = s.sb("raw", [P, 2, LAST + SEQ])
        conv_w = s.sb("conv_w_cols", [P, CONV_W, NGB])
        ps = s.ps("ps_f", [P, 4, 512])
        ps_s = [s.ps(f"ps_s{i}", [P, 512]) for i in range(2)]
        fw_loaded = [s.sem(f"fw_loaded{u}") for u in range(2)]
        out_stored = [s.sem(f"out_stored{u}") for u in range(2)]
        names = ("fw_free", "cw_loaded", "f_ready", "f_free", "s_ready", "s_free", "out_ready",
                 "raw_ready", "conv_step", "zeroed")
        (fw_free, cw_loaded, f_ready, f_free, s_ready, s_free, out_ready, raw_ready,
         conv_step, zeroed) = (s.sem(n) for n in names)
        block = ctx.enter_context(nc.Block())
        NF = NQB + NQIB + NGB
        parts = [(0, NQB, C_Q, 0.125), (NQB, NQIB, C_QI, 1 / 32), (NQB + NQIB, NGB, C_QKV, 1.0)]
        w = d["w_in"].rearrange("(b p) n -> p b n", p=P)
        G0 = NQB + NQIB

        @block.sync
        def _(sp):
            for t in range(CONV_W):
                sp.dma_start(conv_w[:, t, :], d["conv_w"][t].rearrange("(b p) -> p b", p=P)).then_inc(cw_loaded, 16)
            for b0, nb, c0, _ in parts:
                with sp.Fori(0, nb // 2) as j:
                    for u in range(2):
                        i = 2 * j + u
                        sp.wait_ge(fw_free, i + b0 + 1)
                        sp.dma_start(w_blk[:, u, :, :], w[:, :, bass.ds(i * P + c0, P)]).then_inc(fw_loaded[u], 16)

        @block.tensor
        def _(pe):
            pe.sem_inc(fw_free, 2)
            with pe.Fori(0, NF // 2) as j:
                for u in range(2):
                    i = 2 * j + u
                    pe.wait_ge(fw_loaded[u], 16 * j + 16)
                    for n in range(4):
                        pe.wait_ge(f_free, 4 * i + n + 1)
                        for b in range(KB):
                            last = pe.matmul(ps[:, n, :], w_blk[:, u, b, :], hT[:, b, n * 512:(n + 1) * 512],
                                             start=(b == 0), stop=(b == KB - 1))
                        last.then_inc(f_ready, 1)
                    pe.wait_ge(s_free, i + 1)
                    for b in range(KB):
                        last = pe.matmul(ps_s[u][0:SMALL_ROWS, 0:P], h_small[:, b, :], w_blk[:, u, b, :],
                                         start=(b == 0), stop=(b == KB - 1))
                    last.then_inc(s_ready, 1)
                    pe.wait_ge(s_ready, i + 1)
                    pe.sem_inc(fw_free, 1)

        @block.scalar
        def _(act):
            act.sem_inc(f_free, 4)

            def copy_out(i, j, u, scale, first):
                if not first:
                    act.wait_ge(out_stored[u], 16 * j)
                for n in range(4):
                    act.wait_ge(f_ready, 4 * i + n + 1)
                    act.activation(out[:, u, n * 512:(n + 1) * 512], ps[:, n, :], ACT.Copy,
                                   scale=scale).then_inc(f_free, 1)
                act.wait_ge(f_free, 4 * i + 8)
                act.sem_inc(out_ready, 1)

            for u in range(2):
                copy_out(u, 0, u, 0.125, True)
            for b0, nb, _, scale in parts[:2]:
                with act.Fori(1 if b0 == 0 else 0, nb // 2) as j:
                    for u in range(2):
                        copy_out(2 * j + u + b0, j + b0 // 2, u, scale, False)

            def silu(i, u):
                act.wait_ge(conv_step, 4 * (i - G0) + 4)
                act.activation(out[:, u, :], out[:, u, :], ACT.Silu).then_inc(out_ready, 1)

            def copy_raw(i, u):
                for n in range(4):
                    act.wait_ge(f_ready, 4 * i + n + 1)
                    act.activation(raw[:, u, LAST + n * 512:LAST + (n + 1) * 512], ps[:, n, :],
                                   ACT.Copy).then_inc(f_free, 1)
                act.wait_ge(f_free, 4 * i + 8)
                act.sem_inc(raw_ready, 1)

            copy_raw(G0, 0)
            copy_raw(G0 + 1, 1)
            with act.Fori(0, NGB // 2 - 1) as j:
                for u in range(2):
                    silu(2 * j + u + G0, u)
                    copy_raw(2 * j + u + G0 + 2, u)
            silu(NF - 2, 0)
            silu(NF - 1, 1)

        @block.vector
        def _(dve):
            dve.sem_inc(s_free, 2)
            for u in range(2):
                dve.memset(raw[:, u, 0:LAST], 0.0).then_inc(zeroed, 1)
            dve.wait_ge(zeroed, 2)
            dve.wait_ge(cw_loaded, 16 * CONV_W)

            def small(i, u):
                dve.wait_ge(s_ready, i + 1)
                dve.tensor_copy(keep["small"][:, bass.ds(i * P, P)], ps_s[u][0:SMALL_ROWS, 0:P]).then_inc(s_free, 1)

            with dve.Fori(0, G0 // 2) as j:
                for u in range(2):
                    small(2 * j + u, u)
            with dve.Fori(0, NGB // 2) as j:
                for u in range(2):
                    i = 2 * j + u
                    dve.wait_ge(raw_ready, i + 1)
                    dve.wait_ge(out_stored[u], 16 * j + 8 * G0)
                    for t in range(CONV_W):
                        wt = conv_w[:, t, bass.ds(i, 1)]
                        if t == 0:
                            dve.tensor_scalar(out[:, u, :], raw[:, u, 0:SEQ], wt, None, ALU.mult).then_inc(
                                conv_step, 1)
                        else:
                            dve.wait_ge(conv_step, 4 * i + t)
                            dve.scalar_tensor_tensor(out=out[:, u, :], in0=raw[:, u, t:t + SEQ], scalar=wt,
                                                     in1=out[:, u, :], op0=ALU.mult, op1=ALU.add).then_inc(
                                conv_step, 1)
                    small(i + G0, u)

        @block.gpsimd
        def _(pool):
            with pool.Fori(0, NF // 2) as j:
                for u in range(2):
                    i = 2 * j + u
                    pool.wait_ge(out_ready, i + 1)
                    pool.dma_start(d["featT"][bass.ds(i * P, P), :], out[:, u, :]).then_inc(out_stored[u], 16)
            for u in range(2):
                pool.wait_ge(out_stored[u], 8 * NF)


def decay_tables(nc, d, keep):
    with ExitStack() as ctx:
        s = Scope(nc, ctx)
        row = s.sb("a_log_row", [P, G_HEADS])
        dt = s.sb("dt_row", [P, G_HEADS])
        ab = s.sb("gate_inputs", [P, NT + 1, 8])
        y = s.sb("softplus_in", [P, NT + 1, G_HEADS])
        n = s.sb("softplus_neg", [P, NT + 1, G_HEADS])
        last = s.sb("g_last", [P, NT + 1, G_HEADS])
        ps = s.ps("ps_gcum", [P, 2, NT + 1, G_HEADS])
        loaded, dv, ac, summed = s.sem("gate_rows_loaded"), s.sem("gates_dve"), s.sem("gates_act"), s.sem("g_summed")
        block = ctx.enter_context(nc.Block())
        tab = keep["dtab"]
        a, b = ab[:, :, 0:4], ab[:, :, 4:8]

        @block.sync
        def _(sp):
            sp.dma_start(row[:, :], d["a_log"].broadcast_to([P, G_HEADS])).then_inc(loaded, 16)
            sp.dma_start(dt[:, :], d["dt_bias"].broadcast_to([P, G_HEADS])).then_inc(loaded, 16)

        @block.vector
        def _(dve):
            def step(k, ins):
                ins.then_inc(dv, 1)
                dve.wait_ge(dv, k)

            step(1, dve.memset(ab[:, NT, :], 0.0))
            step(2, dve.tensor_copy(ab[:, 0:NT, :], keep["tok"][:, :, T_A:T_A + 8]))
            step(3, dve.tensor_copy(ab[0:NB, NT, :], keep["samp"][:, T_A:T_A + 8]))
            dve.wait_ge(loaded, 32)
            step(4, dve.tensor_tensor(y[:, :, :], a, dt[:, :].unsqueeze(1).broadcast_to([P, NT + 1, G_HEADS]), ALU.add))
            step(5, dve.tensor_scalar(n[:, :, :], y[:, :, :], -1.0, None, ALU.mult))
            step(6, dve.tensor_tensor(n[:, :, :], n[:, :, :], y[:, :, :], ALU.min))
            dve.wait_ge(ac, 3)
            step(7, dve.scalar_tensor_tensor(out=y[:, :, :], in0=y[:, :, :], scalar=0.0, in1=n[:, :, :],
                                             op0=ALU.max, op1=ALU.add))
            step(8, dve.tensor_scalar(row[:, :], row[:, :], -1.0, None, ALU.mult))
            step(9, dve.tensor_tensor(tab[:, :, 7, :], y[:, :, :],
                                      row[:, :].unsqueeze(1).broadcast_to([P, NT + 1, G_HEADS]), ALU.mult))
            dve.wait_ge(ac, 4)
            step(10, dve.tensor_scalar(tab[:, :, 1, :], tab[:, :, 0, :], 1.0, None, ALU.add))
            step(11, dve.reciprocal(tab[:, :, 0, :], tab[:, :, 1, :]))
            step(12, dve.tensor_scalar(tab[:, :, 1, :], tab[:, :, 0, :], -1.0, None, ALU.mult))
            dve.wait_ge(summed, 2)
            step(13, dve.tensor_copy(tab[:, :, 6, :], ps[:, 0, :, :]))
            step(14, dve.tensor_tensor(last[:, :, :], ps[:, 1, :, :], tab[:, :, 6, :], ALU.subtract))
            dve.wait_ge(ac, 7)
            step(15, dve.tensor_tensor(tab[:, :, 2, :], tab[:, :, 1, :], tab[:, :, 4, :], ALU.mult))

        @block.scalar
        def _(act):
            act.wait_ge(loaded, 32)
            act.activation(row[:, :], row[:, :], ACT.Exp).then_inc(ac, 1)
            act.wait_ge(dv, 6)
            act.activation(n[:, :, :], n[:, :, :], ACT.Exp).then_inc(ac, 1)
            act.wait_ge(ac, 2)
            act.activation(n[:, :, :], n[:, :, :], ACT.Ln, bias=1.0).then_inc(ac, 1)
            act.activation(tab[:, :, 0, :], b, ACT.Exp, scale=-1.0).then_inc(ac, 1)
            act.wait_ge(dv, 14)
            act.activation(tab[:, :, 3, :], last[:, :, :], ACT.Exp).then_inc(ac, 1)
            act.activation(tab[:, :, 4, :], tab[:, :, 6, :], ACT.Exp).then_inc(ac, 1)
            act.activation(tab[:, :, 5, :], ps[:, 1, :, :], ACT.Exp).then_inc(ac, 1)

        @block.tensor
        def _(pe):
            pe.wait_ge(dv, 9)
            pe.matmul(ps[:, 0, :, :], keep["upper"][:, :], tab[:, :, 7, :], start=True, stop=True).then_inc(summed, 1)
            pe.matmul(ps[:, 1, :, :], keep["ones"][:, :], tab[:, :, 7, :], start=True, stop=True).then_inc(summed, 1)


LEVELS = 7


def delta_rule(nc, d, keep):
    with ExitStack() as ctx:
        s = Scope(nc, ctx)
        H4 = [P, G_HEADS, P]
        two = lambda name, shape: [s.sb(f"{name}{u}", shape) for u in range(2)]
        qkv_in = two("qkv_in", [P, 12, P])
        gate_in = two("gate_in", [P, 512])
        qkv = two("qkv_tok", [P, 12, P])
        sc = two("chunk_scalars", [P, 8, G_HEADS])
        g_upper = two("g_upper", H4)
        low = two("decay_low", H4)
        up = two("decay_up", H4)
        low_b = two("decay_low_beta", H4)
        sq = two("qk_sq", [P, 8, P])
        norm = two("qk_rnorm", [P, 8])
        qk = two("qk_normed", [P, 8, P])
        v_b = two("v_beta", H4)
        k_bg = two("k_beta_decay", H4)
        k_dec = two("k_decay", H4)
        kqT = two("kqT", [P, 2, 512])
        neg_a = two("neg_a", H4)
        attnT = two("attnT", H4)
        x = two("inv", H4)
        xT = two("invT", H4)
        z = two("z_part", H4)
        wT = two("neg_wT", H4)
        v_new = two("v_new", H4)
        o = two("o_chunk", H4)
        o_sq = two("o_sq", H4)
        o_r = two("o_rnorm", [P, G_HEADS])
        state = s.sb("state", H4)
        gnorm = s.sb("gnorm_row", [P, GD])
        above = s.sb("above", [P, P])
        below = s.sb("below", [P, P])
        ip, js, xr = (s.sb(n, [P, P], I32) for n in ("row_index", "col_index", "index_xor"))
        tri = s.sb("tri", [P, 2, P], I32)
        mask = s.sb("level_mask", [P, 2, LEVELS, P], I32)
        ps = [s.ps(f"ps_g{u}", [P, 4, 512]) for u in range(2)]
        in_loaded = [s.sem(f"qkv_loaded{u}") for u in range(2)]
        g_loaded = [s.sem(f"zg_loaded{u}") for u in range(2)]
        o_stored = [s.sem(f"gdn_stored{u}") for u in range(2)]
        names = ("index_made", "mask_step", "norm_loaded", "in_free", "slot_free", "qkv_turned", "qkv_copied",
                 "sc_ready", "gu_ready", "rows_ready", "diff_ready", "din_ready", "decay_ready", "sq_ready",
                 "sum_ready", "rnorm_ready", "rq_ready", "qk_ready", "vb_ready", "kbg_ready", "kdec_ready",
                 "lowb_ready", "kq_turned", "kq_copied", "gram_ready", "attn_ready", "nega_ready", "attnT_ready",
                 "x_ready", "z_ready", "z_copied", "p_ready", "w_ready", "w_copied", "v_ready", "v_copied",
                 "o_ready", "state_ready", "o_step", "osq_ready", "osum_ready", "or_ready", "on_step", "ssm_stored",
                 "table_ready", "o_free", "seen")
        S = {n: s.sem(n) for n in names}
        block = ctx.enter_context(nc.Block())
        NJ = NT // 2

        def heads(ap):
            return ap.unsqueeze(2).broadcast_to(H4)

        def all_heads(ap):
            return ap.unsqueeze(1).broadcast_to(H4)

        @block.sync
        def _(sp):
            sp.dma_start(gnorm[:, :], d["gdn_norm"].broadcast_to([P, GD])).then_inc(S["norm_loaded"], 16)
            sp.sem_inc(S["o_free"], 2)
            with sp.Fori(0, NJ) as j:
                for u in range(2):
                    c = 2 * j + u
                    sp.wait_ge(S["in_free"], c + 1)
                    sp.dma_start(qkv_in[u][:, :, :], d["featT"][F_QKV:F_ALL, bass.ds(c * P, P)].rearrange(
                        "(b p) t -> p b t", p=P)).then_inc(in_loaded[u], 16)
                    sp.dma_start(gate_in[u][:, :], d["gates"][bass.ds(c * P, P), 512:1024]).then_inc(g_loaded[u], 16)
                for u in range(2):
                    c = 2 * j + u
                    sp.wait_ge(S["on_step"], 4 * c + 4)
                    sp.dma_start(d["mix"][bass.ds(c * P, P), 512:1024], o[u][:, :, :].rearrange(
                        "p h e -> p (h e)")).then_inc(o_stored[u], 16)
                for u in range(2):
                    sp.wait_ge(o_stored[u], 16 * j + 16)
                    sp.sem_inc(S["o_free"], 1)
            sp.wait_ge(S["state_ready"], NT + 1)
            sp.dma_start(d["ssm_prompt"].rearrange("h d e -> d h e"), state[:, :, :]).then_inc(S["ssm_stored"], 16)
            sp.wait_ge(S["ssm_stored"], 16)
            for u in range(2):
                sp.wait_ge(o_stored[u], 16 * NJ)

        @block.gpsimd
        def _(pool):
            pool.iota(ip[:, :], pattern=[[0, P]], base=0, channel_multiplier=1).then_inc(S["index_made"], 1)
            pool.iota(js[:, :], pattern=[[1, P]], base=0, channel_multiplier=0).then_inc(S["index_made"], 1)
            pool.memset(above[:, :], 0.0).then_inc(S["table_ready"], 1)
            pool.memset(below[:, :], 0.0).then_inc(S["table_ready"], 1)
            pool.wait_ge(S["table_ready"], 2)
            pool.affine_select(out=above[:, :], in_=above[:, :], compare_op=ALU.is_gt, fill=-NEG, base=0,
                               pattern=[[-1, P]], channel_multiplier=1).then_inc(S["table_ready"], 1)
            pool.affine_select(out=below[:, :], in_=below[:, :], compare_op=ALU.is_ge, fill=NEG, base=0,
                               pattern=[[1, P]], channel_multiplier=-1).then_inc(S["table_ready"], 1)
            pool.wait_ge(S["norm_loaded"], 16)
            with pool.Fori(0, NJ) as j:
                for u in range(2):
                    c = 2 * j + u
                    pool.wait_ge(S["sum_ready"], c + 1)
                    pool.tensor_tensor(norm[u][:, :], norm[u][:, :], keep["minus_half"][:, 0:8],
                                       ALU.pow).then_inc(S["rnorm_ready"], 1)
                    pool.wait_ge(S["sc_ready"], c + 1)
                    pool.tensor_tensor(v_b[u][:, :, :], qkv[u][:, 8:12, :], heads(sc[u][:, 0, :]),
                                       ALU.mult).then_inc(S["vb_ready"], 1)
                for u in range(2):
                    c = 2 * j + u
                    pool.wait_ge(S["decay_ready"], 2 * c + 2)
                    pool.tensor_tensor(low_b[u][:, :, :], low[u][:, :, :], heads(sc[u][:, 1, :]),
                                       ALU.mult).then_inc(S["lowb_ready"], 1)
                    pool.wait_ge(S["qk_ready"], c + 1)
                    pool.tensor_tensor(k_bg[u][:, :, :], qk[u][:, 4:8, :], heads(sc[u][:, 2, :]),
                                       ALU.mult).then_inc(S["kbg_ready"], 1)
                    pool.tensor_tensor(k_dec[u][:, :, :], qk[u][:, 4:8, :], heads(sc[u][:, 3, :]),
                                       ALU.mult).then_inc(S["kdec_ready"], 1)
                for u in range(2):
                    c = 2 * j + u
                    pool.wait_ge(S["o_step"], 2 * c + 2)
                    pool.tensor_tensor(o_sq[u][:, :, :], o[u][:, :, :], o[u][:, :, :],
                                       ALU.mult).then_inc(S["osq_ready"], 1)
                    pool.wait_ge(S["osum_ready"], c + 1)
                    pool.tensor_tensor(o_r[u][:, :], o_r[u][:, :], keep["minus_half"][:, 0:4],
                                       ALU.pow).then_inc(S["on_step"], 1)
                    pool.wait_ge(S["on_step"], 4 * c + 1)
                    pool.tensor_tensor(o[u][:, :, :], o[u][:, :, :], heads(o_r[u][:, :]),
                                       ALU.mult).then_inc(S["on_step"], 1)
                    pool.wait_ge(S["on_step"], 4 * c + 2)
                    pool.tensor_tensor(o[u][:, :, :], o[u][:, :, :], all_heads(gnorm[:, :]),
                                       ALU.mult).then_inc(S["on_step"], 1)
                    pool.wait_ge(S["on_step"], 4 * c + 3)
                    pool.wait_ge(g_loaded[u], 16 * j + 16)
                    pool.tensor_tensor(o[u][:, :, :], o[u][:, :, :], gate_in[u][:, :].rearrange(
                        "p (h e) -> p h e", h=G_HEADS), ALU.mult).then_inc(S["on_step"], 1)

        @block.vector
        def _(dve):
            dve.wait_ge(S["index_made"], 2)
            step = [0]

            def made(ins):
                step[0] += 1
                ins.then_inc(S["mask_step"], 1)
                dve.wait_ge(S["mask_step"], step[0])

            made(dve.tensor_tensor(xr[:, :], ip[:, :], js[:, :], ALU.bitwise_xor))
            made(dve.tensor_tensor(tri[:, 0, :], ip[:, :], js[:, :], ALU.is_gt))
            made(dve.tensor_tensor(tri[:, 1, :], js[:, :], ip[:, :], ALU.is_gt))
            for lv in range(LEVELS):
                m0 = mask[:, 0, lv, :]
                if lv:
                    made(dve.tensor_scalar(ip[:, :], xr[:, :], lv, None, ALU.logical_shift_right))
                made(dve.tensor_scalar(m0, (ip if lv else xr)[:, :], 1, None, ALU.is_equal))
                made(dve.tensor_tensor(mask[:, 1, lv, :], m0, tri[:, 1, :], ALU.mult))
                made(dve.tensor_tensor(m0, m0, tri[:, 0, :], ALU.mult))
            dve.memset(state[:, :, :], 0.0).then_inc(S["state_ready"], 1)
            dve.wait_ge(S["table_ready"], 4)
            dve.sem_inc(S["slot_free"], 2)
            with dve.Fori(0, NJ) as j:
                for u in range(2):
                    c = 2 * j + u
                    dve.tensor_copy(sc[u][:, :, :], keep["dtab"][:, bass.ds(c, 1), :, :].squeeze(1)).then_inc(
                        S["sc_ready"], 1)
                    dve.wait_ge(S["sc_ready"], c + 1)
                    dve.tensor_tensor(g_upper[u][:, :, :], all_heads(keep["upper"][:, :]), heads(sc[u][:, 7, :]),
                                      ALU.mult).then_inc(S["gu_ready"], 1)
                for u in range(2):
                    c = 2 * j + u
                    dve.wait_ge(S["rows_ready"], c + 1)
                    dve.tensor_tensor(up[u][:, :, :], ps[u][:, 3, :].rearrange("p (h c) -> p h c", h=G_HEADS),
                                      heads(sc[u][:, 6, :]), ALU.subtract).then_inc(S["diff_ready"], 1)
                    dve.wait_ge(S["diff_ready"], c + 1)
                    dve.scalar_tensor_tensor(out=low[u][:, :, :], in0=up[u][:, :, :], scalar=0.0,
                                             in1=all_heads(above[:, :]), op0=ALU.max, op1=ALU.add).then_inc(
                        S["din_ready"], 1)
                    dve.wait_ge(S["din_ready"], 2 * c + 1)
                    dve.scalar_tensor_tensor(out=up[u][:, :, :], in0=up[u][:, :, :], scalar=0.0,
                                             in1=all_heads(below[:, :]), op0=ALU.min, op1=ALU.add).then_inc(
                        S["din_ready"], 1)
                for u in range(2):
                    c = 2 * j + u
                    dve.wait_ge(S["qkv_copied"], c + 1)
                    dve.tensor_tensor(sq[u][:, :, :], qkv[u][:, 0:8, :], qkv[u][:, 0:8, :], ALU.mult).then_inc(
                        S["sq_ready"], 1)
                    dve.wait_ge(S["sq_ready"], 2 * c + 1)
                    dve.tensor_reduce(norm[u][:, :], sq[u][:, :, :], AX.X, ALU.add).then_inc(S["sq_ready"], 1)
                    dve.wait_ge(S["sq_ready"], 2 * c + 2)
                    dve.tensor_scalar(norm[u][:, :], norm[u][:, :], 1e-6, None, ALU.add).then_inc(S["sum_ready"], 1)
                for u in range(2):
                    c = 2 * j + u
                    dve.wait_ge(S["rnorm_ready"], c + 1)
                    dve.tensor_scalar(norm[u][:, 0:4], norm[u][:, 0:4], GD ** -0.5, None, ALU.mult).then_inc(
                        S["rq_ready"], 1)
                    dve.wait_ge(S["rq_ready"], c + 1)
                    dve.tensor_tensor(qk[u][:, :, :], qkv[u][:, 0:8, :],
                                      norm[u][:, :].unsqueeze(2).broadcast_to([P, 8, P]), ALU.mult).then_inc(
                        S["qk_ready"], 1)
                for u in range(2):
                    c = 2 * j + u
                    dve.tensor_copy(x[u][:, :, :], all_heads(keep["ident"][:, :])).then_inc(S["x_ready"], 1)
                    dve.tensor_copy(xT[u][:, :, :], all_heads(keep["ident"][:, :])).then_inc(S["x_ready"], 1)
                    dve.wait_ge(S["gram_ready"], c + 1)
                    dve.wait_ge(S["lowb_ready"], c + 1)
                    dve.tensor_tensor(neg_a[u][:, :, :], ps[u][:, 2, :].rearrange("p (h c) -> p h c", h=G_HEADS),
                                      low_b[u][:, :, :], ALU.mult).then_inc(S["nega_ready"], 1)
                    dve.wait_ge(S["attn_ready"], c + 1)
                    dve.wait_ge(S["decay_ready"], 2 * c + 2)
                    dve.tensor_tensor(attnT[u][:, :, :], ps[u][:, 3, :].rearrange("p (h c) -> p h c", h=G_HEADS),
                                      up[u][:, :, :], ALU.mult).then_inc(S["attnT_ready"], 1)
                XJ = 4 + 4 * LEVELS - 2
                for lv in range(LEVELS):
                    for u in range(2):
                        c = 2 * j + u
                        m0, m1 = all_heads(mask[:, 0, lv, :]), all_heads(mask[:, 1, lv, :])
                        if lv == 0:
                            dve.wait_ge(S["x_ready"], XJ * j + 4 + 2 * u)
                            dve.wait_ge(S["nega_ready"], c + 1)
                            dve.sem_inc(S["seen"], 1)
                            dve.copy_predicated(x[u][:, :, :], m0, neg_a[u][:, :, :]).then_inc(S["x_ready"], 1)
                            dve.wait_ge(S["z_ready"], 2 * LEVELS * j + u + 1)
                            dve.sem_inc(S["seen"], 1)
                            dve.copy_predicated(xT[u][:, :, :], m1, ps[u][:, 0, :].rearrange(
                                "p (h c) -> p h c", h=G_HEADS)).then_inc(S["x_ready"], 1)
                            continue
                        dve.wait_ge(S["p_ready"], 2 * (LEVELS - 1) * j + 2 * (lv - 1) + u + 1)
                        dve.sem_inc(S["seen"], 1)
                        if lv < LEVELS - 1:
                            dve.copy_predicated(x[u][:, :, :], m0, ps[u][:, 1, :].rearrange(
                                "p (h c) -> p h c", h=G_HEADS)).then_inc(S["x_ready"], 1)
                        dve.copy_predicated(xT[u][:, :, :], m1, ps[u][:, 2, :].rearrange(
                            "p (h c) -> p h c", h=G_HEADS)).then_inc(S["x_ready"], 1)
                for u in range(2):
                    c = 2 * j + u
                    dve.wait_ge(S["o_ready"], c + 1)
                    for h in range(G_HEADS):
                        ins = dve.scalar_tensor_tensor(out=state[:, h, :], in0=state[:, h, :],
                                                       scalar=sc[u][:, 5, h:h + 1],
                                                       in1=ps[u][:, 0, h * P:(h + 1) * P], op0=ALU.mult, op1=ALU.add)
                    ins.then_inc(S["state_ready"], 1)
                    if u == 0:
                        dve.wait_ge(S["state_ready"], c + 2)
                    dve.wait_ge(S["o_free"], c + 1)
                    dve.tensor_tensor(o[u][:, :, :], ps[u][:, 2, :].rearrange("p (h c) -> p h c", h=G_HEADS),
                                      heads(sc[u][:, 4, :]), ALU.mult).then_inc(S["o_step"], 1)
                    dve.wait_ge(S["o_step"], 2 * c + 1)
                    dve.tensor_tensor(o[u][:, :, :], o[u][:, :, :],
                                      ps[u][:, 3, :].rearrange("p (h c) -> p h c", h=G_HEADS), ALU.add).then_inc(
                        S["o_step"], 1)
                    dve.wait_ge(S["o_step"], 2 * c + 2)
                    dve.wait_ge(S["state_ready"], c + 2)
                    dve.sem_inc(S["slot_free"], 1)
                for u in range(2):
                    c = 2 * j + u
                    dve.wait_ge(S["osq_ready"], c + 1)
                    dve.tensor_reduce(o_r[u][:, :], o_sq[u][:, :, :], AX.X, ALU.add).then_inc(S["or_ready"], 1)
                    dve.wait_ge(S["or_ready"], c + 1)
                    dve.tensor_scalar(o_r[u][:, :], o_r[u][:, :], 1.0 / GD, EPS, ALU.mult, ALU.add).then_inc(
                        S["osum_ready"], 1)

        @block.scalar
        def _(act):
            with act.Fori(0, NJ) as j:
                for u in range(2):
                    c = 2 * j + u
                    act.wait_ge(S["qkv_turned"], c + 1)
                    act.activation(qkv[u][:, :, :], ps[u][:, 0:3, :].rearrange("p a (b c) -> p (a b) c", c=P),
                                   ACT.Copy).then_inc(S["qkv_copied"], 1)
                for u in range(2):
                    c = 2 * j + u
                    act.wait_ge(S["din_ready"], 2 * c + 2)
                    act.activation(low[u][:, :, :], low[u][:, :, :], ACT.Exp, scale=-1.0).then_inc(
                        S["decay_ready"], 1)
                    act.activation(up[u][:, :, :], up[u][:, :, :], ACT.Exp).then_inc(S["decay_ready"], 1)
                for u in range(2):
                    c = 2 * j + u
                    act.wait_ge(S["kq_turned"], c + 1)
                    act.activation(kqT[u][:, :, :], ps[u][:, 0:2, :], ACT.Copy).then_inc(S["kq_copied"], 1)
                for lv in range(1, LEVELS):
                    for u in range(2):
                        act.wait_ge(S["z_ready"], 2 * LEVELS * j + 2 * lv + u + 1)
                        act.activation(z[u][:, :, :].rearrange("p h c -> p (h c)"), ps[u][:, 0, :],
                                       ACT.Copy).then_inc(S["z_copied"], 1)
                for u in range(2):
                    c = 2 * j + u
                    act.wait_ge(S["w_ready"], c + 1)
                    act.activation(wT[u][:, :, :].rearrange("p h c -> p (h c)"), ps[u][:, 0, :],
                                   ACT.Copy).then_inc(S["w_copied"], 1)
                for u in range(2):
                    c = 2 * j + u
                    act.wait_ge(S["v_ready"], c + 1)
                    act.activation(v_new[u][:, :, :].rearrange("p h c -> p (h c)"), ps[u][:, 1, :],
                                   ACT.Copy).then_inc(S["v_copied"], 1)

        @block.tensor
        def _(pe):
            pe.sem_inc(S["in_free"], 2)
            blk = lambda ap, h: ap[:, h * P:(h + 1) * P]
            with pe.Fori(0, NJ) as j:
                for u in range(2):
                    c = 2 * j + u
                    pe.wait_ge(in_loaded[u], 16 * j + 16)
                    pe.wait_ge(S["slot_free"], c + 1)
                    for b in range(12):
                        last = pe.transpose(ps[u][:, b // 4, (b % 4) * P:(b % 4 + 1) * P], qkv_in[u][:, b, :],
                                            keep["ident"][:, :])
                    last.then_inc(S["qkv_turned"], 1)
                    pe.wait_ge(S["gu_ready"], c + 1)
                    pe.matmul(ps[u][:, 3, :], keep["ones"][:, :], g_upper[u][:, :, :], start=True,
                              stop=True).then_inc(S["rows_ready"], 1)
                    pe.wait_ge(S["qkv_turned"], c + 1)
                    pe.sem_inc(S["in_free"], 1)
                for u in range(2):
                    c = 2 * j + u
                    pe.wait_ge(S["qk_ready"], c + 1)
                    pe.wait_ge(S["qkv_copied"], c + 1)
                    for h in range(G_HEADS):
                        pe.transpose(blk(ps[u][:, 0, :], h), qk[u][:, 4 + h, :], keep["ident"][:, :])
                        last = pe.transpose(blk(ps[u][:, 1, :], h), qk[u][:, h, :], keep["ident"][:, :])
                    last.then_inc(S["kq_turned"], 1)
                for u in range(2):
                    c = 2 * j + u
                    kT, qT = kqT[u][:, 0, :], kqT[u][:, 1, :]
                    pe.wait_ge(S["kq_copied"], c + 1)
                    for h in range(G_HEADS):
                        last = pe.matmul(blk(ps[u][:, 2, :], h), blk(kT, h), blk(kT, h), start=True, stop=True)
                    last.then_inc(S["gram_ready"], 1)
                    pe.wait_ge(S["diff_ready"], c + 1)
                    for h in range(G_HEADS):
                        last = pe.matmul(blk(ps[u][:, 3, :], h), blk(kT, h), blk(qT, h), start=True, stop=True)
                    last.then_inc(S["attn_ready"], 1)
                XJ = 4 + 4 * LEVELS - 2
                for lv in range(LEVELS):
                    for u in range(2):
                        c = 2 * j + u
                        if lv == 0:
                            pe.wait_ge(S["nega_ready"], c + 1)
                            for h in range(G_HEADS):
                                last = pe.transpose(blk(ps[u][:, 0, :], h), neg_a[u][:, h, :], keep["ident"][:, :])
                            last.then_inc(S["z_ready"], 1)
                            continue
                        pe.wait_ge(S["x_ready"], XJ * j + 4 + 4 * (lv - 1) + 2 * u + 2)
                        for h in range(G_HEADS):
                            last = pe.matmul(blk(ps[u][:, 0, :], h), neg_a[u][:, h, :], xT[u][:, h, :], start=True,
                                             stop=True)
                        last.then_inc(S["z_ready"], 1)
                    for u in range(2):
                        if lv == 0:
                            continue
                        pe.wait_ge(S["z_copied"], 2 * (LEVELS - 1) * j + 2 * (lv - 1) + u + 1)
                        for h in range(G_HEADS):
                            if lv < LEVELS - 1:
                                pe.matmul(blk(ps[u][:, 1, :], h), z[u][:, h, :], x[u][:, h, :], start=True,
                                          stop=True)
                            last = pe.matmul(blk(ps[u][:, 2, :], h), x[u][:, h, :], z[u][:, h, :], start=True,
                                             stop=True)
                        last.then_inc(S["p_ready"], 1)
                for u in range(2):
                    c = 2 * j + u
                    pe.wait_ge(S["x_ready"], XJ * j + 4 + 4 * (LEVELS - 1) + u + 1)
                    pe.wait_ge(S["kbg_ready"], c + 1)
                    for h in range(G_HEADS):
                        last = pe.matmul(blk(ps[u][:, 0, :], h), k_bg[u][:, h, :], xT[u][:, h, :], start=True,
                                         stop=True)
                    last.then_inc(S["w_ready"], 1)
                for u in range(2):
                    c = 2 * j + u
                    pe.wait_ge(S["vb_ready"], c + 1)
                    pe.wait_ge(S["w_copied"], c + 1)
                    pe.wait_ge(S["state_ready"], c + 1)
                    for h in range(G_HEADS):
                        pe.matmul(blk(ps[u][:, 1, :], h), xT[u][:, h, :], v_b[u][:, h, :], start=True, stop=False)
                        last = pe.matmul(blk(ps[u][:, 1, :], h), wT[u][:, h, :], state[:, h, :], start=False,
                                         stop=True)
                    last.then_inc(S["v_ready"], 1)
                    for h in range(G_HEADS):
                        pe.matmul(blk(ps[u][:, 2, :], h), blk(kqT[u][:, 1, :], h), state[:, h, :], start=True,
                                  stop=True)
                    pe.wait_ge(S["v_copied"], c + 1)
                    pe.wait_ge(S["kdec_ready"], c + 1)
                    pe.wait_ge(S["attnT_ready"], c + 1)
                    for h in range(G_HEADS):
                        pe.matmul(blk(ps[u][:, 0, :], h), k_dec[u][:, h, :], v_new[u][:, h, :], start=True,
                                  stop=True)
                    for h in range(G_HEADS):
                        last = pe.matmul(blk(ps[u][:, 3, :], h), attnT[u][:, h, :], v_new[u][:, h, :], start=True,
                                         stop=True)
                    last.then_inc(S["o_ready"], 1)


BISECT = 26
NEAR = 2 * P


def bias_tables(nc, d, keep):
    with ExitStack() as ctx:
        s = Scope(nc, ctx)
        hot = s.sb("bucket_hot", [N_BUCKETS, 3 * P])
        rel = s.sb("rel_table_sb", [N_BUCKETS, HEADS])
        vec = s.sb("bias_vec_sb", [HEADS, 3 * P])
        rows = s.sb("bias_rows_sb", [P, 3, HEADS])
        rev = s.sb("bias_rev", [P, HEADS * NEAR])
        flip = s.sb("flip", [P, P])
        ps = s.ps("ps_vec", [HEADS, 3 * P])
        ps_r = s.ps("ps_rows", [P, 3, HEADS])
        ps_n = [s.ps(f"ps_near{i}", [P, 512]) for i in range(2)]
        loaded, made, copied, stored, read, flip0, flip1, flipped, near_ready = (s.sem(n) for n in (
            "bias_loaded", "bias_made", "bias_copied", "bias_stored", "bias_read", "flip_zero", "flip_made",
            "bias_flipped", "near_ready"))
        block = ctx.enter_context(nc.Block())

        @block.gpsimd
        def _(pool):
            pool.memset(flip[:, :], 0.0).then_inc(flip0, 1)
            pool.wait_ge(flip0, 1)
            pool.affine_select(out=flip[:, :], in_=flip[:, :], compare_op=ALU.not_equal, fill=1.0, base=1 - P,
                               pattern=[[1, P]], channel_multiplier=1).then_inc(flip1, 1)

        @block.sync
        def _(sp):
            sp.dma_start(hot[:, :], d["bucket_hot"]).then_inc(loaded, 16)
            sp.dma_start(rel[:, :], d["rel_table"]).then_inc(loaded, 16)
            sp.wait_ge(copied, 2)
            sp.dma_start(d["bias_vec"], vec[:, :]).then_inc(stored, 16)
            sp.dma_start(d["bias_rows"].rearrange("(c p) h -> p c h", p=P), rows[:, :, :]).then_inc(stored, 16)
            sp.wait_ge(stored, 32)
            vec_ap = d["bias_vec"]
            for h in range(HEADS):
                src = bass.AP(vec_ap.tensor, vec_ap.offset + h * 3 * P, [[1, P], [1, NEAR]])
                sp.dma_start(rev[:, h * NEAR:(h + 1) * NEAR], src).then_inc(read, 16)

        @block.tensor
        def _(pe):
            pe.wait_ge(loaded, 32)
            pe.matmul(ps[:, :], rel[:, :], hot[:, :], start=True, stop=True).then_inc(made, 1)
            for c in range(3):
                ins = pe.matmul(ps_r[:, c, :], hot[:, c * P:(c + 1) * P], rel[:, :], start=True, stop=True)
            ins.then_inc(made, 1)
            pe.wait_ge(read, 16 * HEADS)
            pe.wait_ge(flip1, 1)
            for c in range(4):
                if c >= 2:
                    pe.wait_ge(near_ready, c - 1)
                pe.matmul(ps_n[c % 2][:, :], flip[:, :], rev[:, c * 512:(c + 1) * 512], start=True,
                          stop=True).then_inc(flipped, 1)

        @block.vector
        def _(dve):
            dve.wait_ge(made, 2)
            dve.tensor_copy(vec[:, :], ps[:, :]).then_inc(copied, 1)
            dve.tensor_copy(rows[:, :, :], ps_r[:, :, :]).then_inc(copied, 1)
            for c in range(4):
                dve.wait_ge(flipped, c + 1)
                dve.tensor_copy(keep["near"][:, :, :].rearrange("p h j -> p (h j)")[:, c * 512:(c + 1) * 512],
                                ps_n[c % 2][:, :]).then_inc(near_ready, 1)


def sparse_attention(nc, d, keep):
    with ExitStack() as ctx:
        s = Scope(nc, ctx)
        qi = s.sb("qi_tile", [DH, IDX_HEADS, P])
        q = s.sb("q_tile", [DH, HEADS, P])
        gate = s.sb("gate_a", [P, 512])
        wi = s.sb("wi_tile", [P, IDX_HEADS])
        relu = [s.sb(f"relu{i}", [P, 1024]) for i in range(2)]
        score = s.sb("score", [P, SEQ])
        sure = s.sb("sure", [P, SEQ])
        edge = s.sb("edge", [P, SEQ])
        rank = s.sb("rank", [P, SEQ])
        bias = s.sb("mask_bias", [P, P + SEQ])
        near = s.sb("near_mask", [P, NEAR])
        causal = s.sb("causal", [P, 4, 512])
        halves = s.sb("halves", [P, BISECT])
        delta = s.sb("delta", [P, BISECT])
        mids = s.sb("mids", [P, BISECT + 1])
        pred = s.sb("pred", [P, BISECT])
        tmp = s.sb("bound_tmp", [P, BISECT])
        cnt = s.sb("count", [P, 2])
        top = s.sb("row_bound", [P, 4])
        logit = [s.sb(f"logit{i}", [P, SEQ]) for i in range(2)]
        mx = s.sb("row_max", [P, 2, 2])
        nmx = s.sb("neg_max", [P, 2])
        psum_row = s.sb("prob_sum", [P, HEADS])
        rsum = s.sb("prob_rsum", [P, HEADS])
        pT = [s.sb(f"probT{i}", [P, NT, P]) for i in range(2)]
        att = s.sb("att_tile", [P, 512])
        ps_a = [s.ps(f"ps_a{i}", [P, 1024]) for i in range(2)]
        ps_b = [s.ps(f"ps_b{i}", [P, 512]) for i in range(2)]
        ps_v = s.ps("ps_v", [P, 512])
        names = ("qi_loaded", "q_loaded", "gate_loaded", "scores_ready", "relu_done", "acc_done", "wi_ready",
                 "top_step", "logits_ready", "logits_done", "max_ready", "p_ready", "pT_ready", "pT_copied",
                 "pv_ready", "att_done", "att_stored", "table_made", "seen", "idx_done", "qk_done", "near_step", "rsum_ready", "att_room")
        S = {n: s.sem("sa_" + n) for n in names}
        block = ctx.enter_context(nc.Block())

        GROUPS = [512 * (g + 1) for g in range(4)]
        U = [-(-w // 1024) for w in GROUPS]
        idx_base = [sum(4 * IDX_HEADS * x for x in U[:g]) for g in range(4)]
        qk_base = [sum(4 * HEADS * x for x in U[:g]) for g in range(4)]
        pt_base = [sum(4 * HEADS * (x // 512) for x in GROUPS[:g]) for g in range(4)]

        def unit_cols(g, n):
            return 1024 * n, min(GROUPS[g], 1024 * (n + 1))

        def run(eng, step):
            step((0, 0), None)
            for g in range(4):
                with eng.Fori(0, 3) as r:
                    step((g, r + 1), (g, r))
                step((g + 1, 0) if g < 3 else None, (g, 3))

        @block.sync
        def _(sp):
            def step(a, b):
                if a:
                    g, r = a
                    t = 4 * g + r
                    if b:
                        sp.wait_ge(S["idx_done"], t)
                    sp.dma_start(qi[:, :, :], d["featT"][F_QI:F_QKV, bass.ds(t * P, P)].rearrange(
                        "(h d) t -> d h t", d=DH)).then_inc(S["qi_loaded"], 16)
                if b:
                    g, r = b
                    t = 4 * g + r
                    sp.wait_ge(S["qk_done"], t + 1)
                    sp.wait_ge(S["att_done"], 2 * t + 2)
                    sp.dma_start(q[:, :, :], d["featT"][F_Q:F_QI, bass.ds(t * P, P)].rearrange(
                        "(h d) t -> d h t", d=DH)).then_inc(S["q_loaded"], 16)
                    sp.dma_start(gate[:, :], d["gates"][bass.ds(t * P, P), 0:512]).then_inc(S["gate_loaded"], 16)
            run(sp, step)

        @block.gpsimd
        def _(pool):
            pool.memset(causal[:, :, :], 0.0).then_inc(S["table_made"], 1)
            for k in range(BISECT):
                pool.memset(halves[:, k:k + 1], 2.0 ** -k).then_inc(S["table_made"], 1)
            pool.wait_ge(S["table_made"], 1 + BISECT)
            for r in range(4):
                pool.affine_select(out=causal[:, r, :], in_=causal[:, r, :], compare_op=ALU.is_ge, fill=NEG,
                                   base=P * r, pattern=[[-1, 512]], channel_multiplier=1).then_inc(
                    S["table_made"], 1)

            def step(a, b):
                if b:
                    g, r = b
                    t = 4 * g + r
                    pool.wait_ge(S["att_done"], 2 * t + 4)
                    pool.dma_start(d["mix"][bass.ds(t * P, P), 0:512], att[:, :]).then_inc(S["att_stored"], 16)
                    pool.wait_ge(S["att_stored"], 16 * t + 16)
                    pool.sem_inc(S["att_room"], 1)
            pool.sem_inc(S["att_room"], 1)
            run(pool, step)

        @block.tensor
        def _(pe):
            def step(a, b):
                if a:
                    g, r = a
                    t = 4 * g + r
                    k0 = idx_base[g] + r * (IDX_HEADS * U[g])
                    pe.wait_ge(S["qi_loaded"], 16 * t + 16)
                    if b:
                        pe.wait_ge(S["logits_done"], qk_base[b[0]] + b[1] * (HEADS * U[b[0]]) + 1)
                        pe.wait_ge(S["relu_done"], k0)
                    for h in range(IDX_HEADS):
                        for n in range(U[g]):
                            k = h * U[g] + n
                            c0, c1 = unit_cols(g, n)
                            if k >= 2:
                                pe.wait_ge(S["relu_done"], k0 + k - 1)
                            for c in range(c0, c1, 512):
                                last = pe.matmul(ps_a[k % 2][:, c - c0:c - c0 + 512], qi[:, h, :],
                                                 keep["kidxT"][:, c:c + 512], start=True, stop=True)
                            last.then_inc(S["scores_ready"], 1)
                    pe.wait_ge(S["scores_ready"], k0 + IDX_HEADS * U[g])
                    pe.sem_inc(S["idx_done"], 1)
                if not b:
                    return
                g, r = b
                t = 4 * g + r
                k0 = qk_base[g] + r * (HEADS * U[g])
                nblk = GROUPS[g] // P
                nq = nblk // 4
                q0 = pt_base[g] + r * (HEADS * nq)
                pe.wait_ge(S["q_loaded"], 16 * t + 16)
                if a:
                    ga, ra = a
                    pe.wait_ge(S["relu_done"], idx_base[ga] + ra * (IDX_HEADS * U[ga]) + IDX_HEADS * U[ga])

                def qk(h):
                    for n in range(U[g]):
                        k = h * U[g] + n
                        c0, c1 = unit_cols(g, n)
                        if k >= 2:
                            pe.wait_ge(S["logits_done"], k0 + k)
                        for c in range(c0, c1, 512):
                            last = pe.matmul(ps_a[k % 2][:, c - c0:c - c0 + 512], q[:, h, :],
                                             keep["keyT"][:, h // 4, c:c + 512], start=True, stop=True)
                        last.then_inc(S["logits_ready"], 1)

                def turn(h):
                    pe.wait_ge(S["p_ready"], HEADS * t + h + 1)
                    for n in range(nq):
                        m = h * nq + n
                        pe.wait_ge(S["pT_copied"], q0 + m + 1)
                        for i in range(4):
                            last = pe.transpose(ps_b[m % 2][:, i * P:(i + 1) * P],
                                                logit[h % 2][:, (4 * n + i) * P:(4 * n + i + 1) * P],
                                                keep["ident"][:, :])
                        last.then_inc(S["pT_ready"], 1)

                def pv(h):
                    pe.wait_ge(S["pT_copied"], q0 + h * nq + nq + 2)
                    v0 = T_V + DH * (h // 4)
                    for i in range(nblk):
                        last = pe.matmul(ps_v[:, h * DH:(h + 1) * DH], pT[h % 2][:, i, :],
                                         keep["tok"][:, i, v0:v0 + DH], start=(i == 0), stop=(i == nblk - 1))
                    last.then_inc(S["pv_ready"], 1)

                qk(0)
                for h in range(HEADS):
                    if h + 1 < HEADS:
                        qk(h + 1)
                    if h == HEADS - 1:
                        pe.wait_ge(S["logits_ready"], k0 + HEADS * U[g])
                        pe.sem_inc(S["qk_done"], 1)
                    turn(h)
                    if h == 0:
                        pe.wait_ge(S["att_done"], 2 * t + 2)
                    pv(h)

            pe.sem_inc(S["qk_done"], 1)
            pe.sem_inc(S["pv_ready"], 2)
            run(pe, step)

        @block.scalar
        def _(act):
            def step(a, b):
                if a:
                    g, r = a
                    k0 = idx_base[g] + r * (IDX_HEADS * U[g])
                    for h in range(IDX_HEADS):
                        for n in range(U[g]):
                            k = h * U[g] + n
                            c0, c1 = unit_cols(g, n)
                            act.wait_ge(S["scores_ready"], k0 + k + 1)
                            if b or k >= 2:
                                act.wait_ge(S["acc_done"], k0 + k - 1)
                            act.activation(relu[k % 2][:, 0:c1 - c0], ps_a[k % 2][:, 0:c1 - c0],
                                           ACT.Relu).then_inc(S["relu_done"], 1)
                if not b:
                    return
                g, r = b
                t = 4 * g + r
                w = GROUPS[g]
                nq = w // 512
                q0 = pt_base[g] + r * (HEADS * nq)

                def exps(h):
                    act.wait_ge(S["max_ready"], HEADS * t + h + 1)
                    act.activation(logit[h % 2][:, 0:w], logit[h % 2][:, 0:w], ACT.Exp, bias=nmx[:, h % 2:h % 2 + 1],
                                   accum_out=psum_row[:, h:h + 1]).then_inc(S["p_ready"], 1)

                def copies(h):
                    for n in range(nq):
                        m = h * nq + n
                        act.wait_ge(S["pT_ready"], q0 + m + 1)
                        if n == 0:
                            act.wait_ge(S["pv_ready"], HEADS * t + h + 1)
                        act.activation(pT[h % 2][:, 4 * n:4 * n + 4, :].rearrange("p a b -> p (a b)"),
                                       ps_b[m % 2][:, :], ACT.Copy).then_inc(S["pT_copied"], 1)

                for h in range(HEADS):
                    exps(h)
                    copies(h)

            act.sem_inc(S["pT_copied"], 2)
            run(act, step)

        @block.vector
        def _(dve):
            dve.sem_inc(S["att_done"], 2)
            dve.sem_inc(S["logits_done"], 1)
            dve.memset(mids[:, 0:1], 0.0).then_inc(S["seen"], 1)
            dve.memset(bias[:, 0:P], 0.0).then_inc(S["seen"], 1)
            dve.wait_ge(S["table_made"], 5 + BISECT)

            def step(a, b):
                local = [0]
                base = [None]

                def link(ins):
                    local[0] += 1
                    ins.then_inc(S["top_step"], 1)
                    dve.wait_ge(S["top_step"], base[0] + local[0])

                if a:
                    g, r = a
                    t = 4 * g + r
                    base[0] = t * TOP_STEPS
                    w = GROUPS[g]
                    k0 = idx_base[g] + r * (IDX_HEADS * U[g])
                    dve.tensor_copy(wi[:, :], keep["tok"][:, bass.ds(t, 1), T_WI:T_WI + IDX_HEADS].squeeze(1)
                                    if not isinstance(t, int) else
                                    keep["tok"][:, t, T_WI:T_WI + IDX_HEADS]).then_inc(S["wi_ready"], 1)
                    dve.wait_ge(S["wi_ready"], t + 1)
                    for h in range(IDX_HEADS):
                        for n in range(U[g]):
                            k = h * U[g] + n
                            c0, c1 = unit_cols(g, n)
                            dve.wait_ge(S["relu_done"], k0 + k + 1)
                            if h == 0:
                                ins = dve.tensor_scalar(score[:, c0:c1], relu[k % 2][:, 0:c1 - c0], wi[:, 0:1], None,
                                                        ALU.mult)
                            else:
                                dve.wait_ge(S["acc_done"], k0 + k + 1 - U[g])
                                ins = dve.scalar_tensor_tensor(out=score[:, c0:c1], in0=relu[k % 2][:, 0:c1 - c0],
                                                               scalar=wi[:, h:h + 1], in1=score[:, c0:c1],
                                                               op0=ALU.mult, op1=ALU.add)
                            ins.then_inc(S["acc_done"], 1)
                    dve.wait_ge(S["acc_done"], k0 + IDX_HEADS * U[g])
                    link(dve.tensor_reduce(top[:, 0:1], score[:, 0:w], AX.X, ALU.max, apply_absolute_value=True))
                    mask = causal[:, r, :] if isinstance(r, int) else causal[:, bass.ds(r, 1), :].squeeze(1)
                    link(dve.tensor_tensor(score[:, w - 512:w], score[:, w - 512:w], mask, ALU.add))
                    link(dve.tensor_scalar(delta[:, :], halves[:, :], top[:, 0:1], None, ALU.mult))

                def bisect(k):
                    w = GROUPS[a[0]]
                    link(dve.tensor_scalar(rank[:, 0:w], score[:, 0:w], mids[:, k:k + 1], None, ALU.is_ge, ALU.add,
                                           accum_out=cnt[:, 0:1]))
                    link(dve.tensor_scalar(pred[:, k:k + 1], cnt[:, 0:1], float(TOPK), 0.5, ALU.is_ge, ALU.subtract))
                    link(dve.scalar_tensor_tensor(out=mids[:, k + 1:k + 2], in0=pred[:, k:k + 1],
                                                  scalar=delta[:, k:k + 1], in1=mids[:, k:k + 1], op0=ALU.mult,
                                                  op1=ALU.add))

                def logits(h):
                    g, r = b
                    t = 4 * g + r
                    w = GROUPS[g]
                    k0 = qk_base[g] + r * (HEADS * U[g])
                    region = bias[:, bass.ds(t * P, NEAR)] if not isinstance(t, int) else \
                        bias[:, t * P:t * P + NEAR]
                    if h == 0:
                        dve.tensor_copy(near[:, :], region).then_inc(S["near_step"], 1)
                        dve.wait_ge(S["near_step"], (HEADS + 1) * t + 1)
                    dve.tensor_tensor(region, near[:, :], keep["near"][:, h, :], ALU.add).then_inc(
                        S["near_step"], 1)
                    dve.wait_ge(S["near_step"], (HEADS + 1) * t + h + 2)
                    dve.wait_ge(S["pv_ready"], HEADS * t + h + 1)
                    for n in range(U[g]):
                        c0, c1 = unit_cols(g, n)
                        dve.wait_ge(S["logits_ready"], k0 + h * U[g] + n + 1)
                        dve.sem_inc(S["seen"], 1)
                        dve.tensor_tensor_reduce(out=logit[h % 2][:, c0:c1], in0=ps_a[(h * U[g] + n) % 2][:, 0:c1 - c0],
                                                 in1=bias[:, P + c0:P + c1], scale=1.0, scalar=NEG * 10, op0=ALU.add,
                                                 op1=ALU.max, accum_out=mx[:, h % 2, n:n + 1]).then_inc(
                            S["logits_done"], 1)
                    dve.wait_ge(S["logits_done"], k0 + (h + 1) * U[g] + 1)
                    dve.tensor_reduce(nmx[:, h % 2:h % 2 + 1], mx[:, h % 2, 0:U[g]], AX.X, ALU.max,
                                      negate=True).then_inc(S["max_ready"], 1)

                for h in range(HEADS):
                    if b:
                        logits(h)
                    if a:
                        for k in range(h * BISECT // HEADS, (h + 1) * BISECT // HEADS):
                            bisect(k)
                if b:
                    g, r = b
                    t = 4 * g + r
                    dve.wait_ge(S["p_ready"], HEADS * t + HEADS)
                    dve.reciprocal(rsum[:, :], psum_row[:, :]).then_inc(S["rsum_ready"], 1)
                    dve.wait_ge(S["rsum_ready"], t + 1)
                    dve.wait_ge(S["pv_ready"], HEADS * t + HEADS + 2)
                    dve.wait_ge(S["att_room"], t + 1)
                    dve.tensor_tensor(att[:, :].rearrange("p (h e) -> p h e", h=HEADS),
                                      ps_v[:, :].rearrange("p (h e) -> p h e", h=HEADS),
                                      rsum[:, :].unsqueeze(2).broadcast_to([P, HEADS, DH]), ALU.mult).then_inc(
                        S["att_done"], 1)
                    dve.wait_ge(S["att_done"], 2 * t + 3)
                    dve.wait_ge(S["gate_loaded"], 16 * t + 16)
                    dve.tensor_tensor(att[:, :], att[:, :], gate[:, :], ALU.mult).then_inc(S["att_done"], 1)
                if a:
                    g, r = a
                    w = GROUPS[g]
                    link(dve.tensor_scalar(tmp[:, :], pred[:, :], 0.5, -NEG, ALU.subtract, ALU.mult))
                    link(dve.tensor_tensor(tmp[:, :], tmp[:, :], mids[:, 0:BISECT], ALU.add))
                    link(dve.tensor_reduce(top[:, 1:2], tmp[:, :], AX.X, ALU.max))
                    link(dve.tensor_scalar(top[:, 2:3], top[:, 0:1], -1.0, None, ALU.mult))
                    link(dve.tensor_tensor(top[:, 1:2], top[:, 1:2], top[:, 2:3], ALU.max))
                    link(dve.tensor_scalar(tmp[:, :], pred[:, :], 0.5, -NEG, ALU.add, ALU.mult))
                    link(dve.tensor_tensor(tmp[:, :], tmp[:, :], mids[:, 0:BISECT], ALU.add))
                    link(dve.tensor_reduce(top[:, 2:3], tmp[:, :], AX.X, ALU.min))
                    link(dve.tensor_tensor(top[:, 2:3], top[:, 2:3], top[:, 0:1], ALU.min))
                    link(dve.tensor_scalar(sure[:, 0:w], score[:, 0:w], top[:, 2:3], None, ALU.is_gt, ALU.add,
                                           accum_out=cnt[:, 0:1]))
                    link(dve.scalar_tensor_tensor(out=edge[:, 0:w], in0=score[:, 0:w], scalar=top[:, 1:2],
                                                  in1=sure[:, 0:w], op0=ALU.is_ge, op1=ALU.subtract))
                    link(dve.tensor_scalar(top[:, 3:4], cnt[:, 0:1], -1.0, float(TOPK), ALU.mult, ALU.add))
                    link(dve.tensor_tensor_scan(rank[:, 0:w], edge[:, 0:w], edge[:, 0:w], 0.0, ALU.add, ALU.max))
                    link(dve.scalar_tensor_tensor(out=edge[:, 0:w], in0=rank[:, 0:w], scalar=top[:, 3:4],
                                                  in1=edge[:, 0:w], op0=ALU.is_le, op1=ALU.mult))
                    link(dve.scalar_tensor_tensor(out=edge[:, 0:w], in0=sure[:, 0:w], scalar=1.0,
                                                  in1=edge[:, 0:w], op0=ALU.subtract, op1=ALU.add))
                    link(dve.tensor_scalar(bias[:, P:P + w], edge[:, 0:w], -NEG, None, ALU.mult))
                    assert local[0] == TOP_STEPS, local[0]

            run(dve, step)


TOP_STEPS = 3 + 3 * BISECT + 16


def output_projection(nc, d, keep):
    with ExitStack() as ctx:
        s = Scope(nc, ctx)
        w = s.sb("w_out_sb", [P, KB, D_MODEL])
        fin = s.sb("norm_final_row", [P, D_MODEL])
        mix = s.sb("mix_in", [P, 2, D_MODEL])
        x = s.sb("res_in", [P, 2, D_MODEL])
        mixT = s.sb("mixT", [P, 2, KB, P])
        y = s.sb("y_tile", [P, 2, D_MODEL])
        sq = s.sb("y_sq", [P, 2, D_MODEL])
        r = s.sb("y_rnorm", [P, 2])
        ps_t = s.ps("ps_mixT", [P, KB, P])
        ps_o = [s.ps(f"ps_y{i}", [P, D_MODEL]) for i in range(2)]
        mix_loaded = [s.sem(f"mix_loaded{u}") for u in range(2)]
        y_stored = [s.sem(f"y_stored{u}") for u in range(2)]
        names = ("w_loaded", "in_free", "mix_turned", "mixT_copied", "proj_ready", "y_ready", "ysum_ready",
                 "yr_ready", "y_step", "ym_ready")
        S = {n: s.sem("o_" + n) for n in names}
        block = ctx.enter_context(nc.Block())
        NJ = NT // 2

        def tiles(eng, tile, first=None):
            if first:
                first()
            with eng.Fori(1 if first else 0, NJ) as j:
                for u in range(2):
                    tile(2 * j + u, j, u, P)
            tile(NT, NJ, 0, NB)

        @block.sync
        def _(sp):
            def tile(t, j, u, rows):
                sp.wait_ge(S["in_free"], t + 1)
                src = d["x_sample"] if rows == NB else d["x_prompt"][bass.ds(t * P, P), :]
                sp.dma_start(mix[0:rows, u, :], d["mix"][bass.ds(t * P, rows), :]).then_inc(mix_loaded[u], 16)
                sp.dma_start(x[0:rows, u, :], src).then_inc(mix_loaded[u], 16)

            sp.dma_start(w[:, :, :], d["w_out"].rearrange("(b p) n -> p b n", p=P)).then_inc(S["w_loaded"], 16)
            sp.dma_start(fin[:, :], d["norm_final"].unsqueeze(0).broadcast_to([P, D_MODEL])).then_inc(S["w_loaded"], 16)
            tiles(sp, tile)

        @block.tensor
        def _(pe):
            def turn(t, j, u, rows, first=False):
                pe.wait_ge(mix_loaded[u], 32 * j + 32)
                if not first:
                    pe.wait_ge(S["mixT_copied"], t)
                for b in range(KB):
                    last = pe.transpose(ps_t[:, b, 0:rows], mix[0:rows, u, b * P:(b + 1) * P],
                                        keep["ident"][0:rows, 0:rows])
                last.then_inc(S["mix_turned"], 1)

            def products(t, u, rows):
                pe.wait_ge(S["mixT_copied"], t + 1)
                pe.wait_ge(S["y_ready"], t + 1)
                for c in range(2):
                    for b in range(KB):
                        last = pe.matmul(ps_o[u][0:rows, c * 512:(c + 1) * 512], mixT[:, u, b, 0:rows],
                                         w[:, b, c * 512:(c + 1) * 512], start=(b == 0), stop=(b == KB - 1))
                last.then_inc(S["proj_ready"], 1)

            turn(0, 0, 0, P, first=True)
            pe.wait_ge(S["w_loaded"], 32)
            with pe.Fori(0, NJ - 1) as j:
                turn(2 * j + 1, j, 1, P)
                products(2 * j, 0, P)
                turn(2 * j + 2, j + 1, 0, P)
                products(2 * j + 1, 1, P)
            turn(NT - 1, NJ - 1, 1, P)
            products(NT - 2, 0, P)
            turn(NT, NJ, 0, NB)
            products(NT - 1, 1, P)
            products(NT, 0, NB)

        @block.scalar
        def _(act):
            def tile(t, j, u, rows, first=False):
                act.wait_ge(S["mix_turned"], t + 1)
                if not first:
                    act.wait_ge(S["proj_ready"], t - 1)
                act.activation(mixT[:, u, :, 0:rows], ps_t[:, :, 0:rows], ACT.Copy).then_inc(S["mixT_copied"], 1)

            def first():
                tile(0, 0, 0, P, True)
                tile(1, 0, 1, P, True)

            tiles(act, tile, first)

        @block.vector
        def _(dve):
            dve.sem_inc(S["y_ready"], 2)
            dve.sem_inc(S["in_free"], 2)
            dve.wait_ge(S["w_loaded"], 32)

            def tile(t, j, u, rows, first=False):
                dve.wait_ge(S["proj_ready"], t + 1)
                dve.wait_ge(mix_loaded[u], 32 * j + 32)
                if not first:
                    dve.wait_ge(y_stored[u], 16 * j)
                dve.tensor_tensor(y[0:rows, u, :], ps_o[u][0:rows, :], x[0:rows, u, :], ALU.add).then_inc(
                    S["y_ready"], 1)
                dve.wait_ge(S["y_ready"], t + 3)
                dve.sem_inc(S["in_free"], 1)
                dve.tensor_tensor(sq[0:rows, u, :], y[0:rows, u, :], y[0:rows, u, :], ALU.mult).then_inc(
                    S["ysum_ready"], 1)
                dve.wait_ge(S["ysum_ready"], 2 * t + 1)
                dve.tensor_reduce(r[0:rows, u:u + 1], sq[0:rows, u, :], AX.X, ALU.add).then_inc(S["ysum_ready"], 1)
                dve.wait_ge(S["ysum_ready"], 2 * t + 2)
                dve.tensor_scalar(r[0:rows, u:u + 1], r[0:rows, u:u + 1], 1.0 / D_MODEL, EPS, ALU.mult,
                                  ALU.add).then_inc(S["ym_ready"], 1)
                dve.wait_ge(S["yr_ready"], t + 1)
                dve.scalar_tensor_tensor(out=y[0:rows, u, :], in0=y[0:rows, u, :], scalar=r[0:rows, u:u + 1],
                                         in1=fin[0:rows, :], op0=ALU.mult, op1=ALU.mult).then_inc(S["y_step"], 1)

            def first():
                tile(0, 0, 0, P, True)
                tile(1, 0, 1, P, True)

            tiles(dve, tile, first)

        @block.gpsimd
        def _(pool):
            def tile(t, j, u, rows):
                pool.wait_ge(S["ym_ready"], t + 1)
                pool.tensor_tensor(r[0:rows, u:u + 1], r[0:rows, u:u + 1], keep["minus_half"][0:rows, 0:1],
                                   ALU.pow).then_inc(S["yr_ready"], 1)
                pool.wait_ge(S["y_step"], t + 1)
                dst = d["y_sample"] if rows == NB else d["y_prompt"][bass.ds(t * P, P), :]
                pool.dma_start(dst, y[0:rows, u, :]).then_inc(y_stored[u], 16)

            tiles(pool, tile)
            pool.wait_ge(y_stored[0], 16 * (NJ + 1))
            pool.wait_ge(y_stored[1], 16 * NJ)


PAIRS = NB // 2
COLS = PAGE + 1


class Sems(dict):

    def __init__(self, scope, prefix):
        self.scope, self.prefix = scope, prefix

    def __missing__(self, name):
        self[name] = self.scope.sem(self.prefix + name)
        return self[name]


class Chain:

    def __init__(self, eng, sem):
        self.eng, self.sem, self.n = eng, sem, 0

    def __call__(self, ins):
        self.n += 1
        ins.then_inc(self.sem, 1)
        self.eng.wait_ge(self.sem, self.n)


def decode_tables(nc, keep, T):
    with ExitStack() as ctx:
        s = Scope(nc, ctx)
        S = Sems(s, "dt_")
        block = ctx.enter_context(nc.Block())

        @block.gpsimd
        def _(pool):
            link = Chain(pool, S["step"])

            def select(ap, op, fill, base, pattern, cm):
                link(pool.affine_select(out=ap, in_=ap, compare_op=op, fill=fill, base=base, pattern=pattern,
                                        channel_multiplier=cm))

            link(pool.memset(T["seq_of"][:, :, :], 0.0))
            select(T["seq_of"][:, :, :], ALU.not_equal, 1.0, 0, [[-1, NB], [0, N_PAGES]], 1)
            link(pool.memset(T["last_page"][:, :, :], 0.0))
            select(T["last_page"][:, :, :], ALU.not_equal, 1.0, 1 - N_PAGES, [[-N_PAGES, 2], [0, P]], 1)
            link(pool.memset(T["same_half"][:, :, :], 1.0))
            select(T["same_half"][:, :, :], ALU.is_ge, 0.0, 0, [[-N_PAGES, 2], [0, N_PAGES]], 1)
            select(T["same_half"][:, :, :], ALU.is_ge, 0.0, N_PAGES - 1, [[N_PAGES, 2], [0, N_PAGES]], -1)
            link(pool.tensor_copy(T["before"][:, :], T["same_half"][:, :, :].rearrange("k s p -> k (s p)")))
            select(T["before"][:, :], ALU.is_gt, 0.0, 0, [[1, P]], -1)
            link(pool.memset(T["new_mask"][:, :], NEG))
            select(T["new_mask"][:, :], ALU.not_equal, 0.0, 1 - N_PAGES, [[0, 1]], 1)
            select(T["new_mask"][:, :], ALU.not_equal, 0.0, 1 - P, [[0, 1]], 1)
            link(pool.memset(T["half_base"][:, :], float(TOPK)))
            select(T["half_base"][:, :], ALU.is_ge, 0.0, -N_PAGES, [[0, 1]], 1)
            link(pool.iota(T["iota_i"][:, :], pattern=[[1, COLS]], base=0, channel_multiplier=0))
            link(pool.tensor_copy(T["iota_c"][:, :], T["iota_i"][:, :]))
            link(pool.iota(T["page_i"][:, :], pattern=[[0, 1]], base=0, channel_multiplier=PAGE))
            link(pool.tensor_copy(T["page_f"][:, :], T["page_i"][:, :]))
            link(pool.tensor_scalar(T["page_rel"][:, :], T["half_base"][:, :], float(PAST // TOPK),
                                    float(PAST + 1 - 2 * P), ALU.mult, ALU.add))
            link(pool.tensor_tensor(T["page_rel"][:, :], T["page_f"][:, :], T["page_rel"][:, :], ALU.subtract))


def decode_indexer(nc, d, keep, T):
    with ExitStack() as ctx:
        s = Scope(nc, ctx)
        S = Sems(s, "di_")
        kidx = [s.sb(f"kidx_pages{i}", [P, PAGE * DH]) for i in range(2)]
        kT = [s.sb(f"kidx_turned{i}", [P, 512]) for i in range(2)]
        q_blk = s.sb("qi_block", [P, NB, 2, IDX_HEADS])
        w_row = s.sb("wi_rows", [P, IDX_HEADS])
        prod = s.sb("relu_weighted", [P, 64, IDX_HEADS])
        pg = s.sb("page_rows", [P, PAIRS], I32)
        new = s.sb("new_prod", [NB, IDX_HEADS, DH])
        new_h = s.sb("new_heads", [NB, IDX_HEADS])
        new_s = s.sb("new_score", [NB, 1])
        qi2 = s.sb("qi_twice", [NB, IDX_HEADS, 2, DH])
        ps_t = [s.ps(f"ps_kt{i}", [P, 512]) for i in range(2)]
        ps_s = [s.ps(f"ps_ks{i}", [P, 1024]) for i in range(2)]
        ps_w = s.ps("ps_wi", [P, 512])
        ps_q = s.ps("ps_qi", [P, 512])
        block = ctx.enter_context(nc.Block())
        k_loaded = [S[f"kidx_loaded{i}"] for i in range(2)]

        @block.sync
        def _(sp):
            for n in range(PAIRS):
                sp.dma_start(pg[:, n:n + 1], d["page_table"][2 * n:2 * n + 2, :].rearrange(
                    "s (g o) -> (s g) o", o=1)).then_inc(S["pages_loaded"], 16)

        @block.gpsimd
        def _(pool):
            pool.wait_ge(S["pages_loaded"], 16 * PAIRS)
            for n in range(PAIRS):
                if n >= 2:
                    pool.wait_ge(S["turned"], 16 * (n - 1))
                pool.indirect_dma_start(kidx[n % 2][:, :], None, d["kidx_by_page"],
                                        bass.IndirectOffsetOnAxis(ap=pg[:, n:n + 1].bitcast(U32), axis=0)).then_inc(
                    k_loaded[n % 2], 16)

        @block.tensor
        def _(pe):
            pe.wait_ge(S["q_twice"], 2)
            for h in range(IDX_HEADS):
                last = pe.matmul(ps_q[:, h * NB:(h + 1) * NB], qi2[:, h, :, :],
                                 keep["ident"][0:NB, 0:NB], start=True, stop=True)
            last.then_inc(S["q_turned"], 1)
            for n in range(PAIRS):
                pe.wait_ge(k_loaded[n % 2], 16 * (n // 2 + 1))
                if n:
                    pe.wait_ge(S["w_copied"], n)
                pe.matmul(ps_w[:, 0:IDX_HEADS], T["seq_of"][:, 2 * n:2 * n + 2, :],
                          keep["samp"][:, T_WI:T_WI + IDX_HEADS], start=True, stop=True).then_inc(S["w_ready"], 1)
                if n == 0:
                    pe.wait_ge(S["q_block_ready"], 3)

                def turn(g):
                    m = 16 * n + g
                    if m >= 2:
                        pe.wait_ge(S["turn_copied"], m - 1)
                    for i in range(4):
                        c = (4 * g + i) * P
                        last = pe.transpose(ps_t[m % 2][:, i * P:(i + 1) * P], kidx[n % 2][:, c:c + P],
                                            keep["ident"][:, :])
                    last.then_inc(S["turned"], 1)

                def scores(g):
                    m = 16 * n + g
                    pe.wait_ge(S["turn_copied"], m + 1)
                    b = m // 8
                    if g % 8 == 0 and b >= 2:
                        pe.wait_ge(S["weighted"], b - 1)
                    for i in range(4):
                        c = ((4 * g + i) % 32) * 32
                        for half in range(2):
                            last = pe.matmul(ps_s[b % 2][64 * half:64 * half + 64, c:c + 32],
                                             kT[m % 2][:, i * P + 64 * half:i * P + 64 * half + 64],
                                             q_blk[:, 2 * n + half, :, :], start=True, stop=True)
                    last.then_inc(S["scored"], 1)

                for g in range(16):
                    turn(g)
                    if g:
                        scores(g - 1)
                scores(15)
            pe.wait_ge(S["new_ready"], 1)
            for n in range(PAIRS):
                last = pe.matmul(ps_q[:, 256 + n:257 + n], T["seq_of"][:, 2 * n:2 * n + 2, :], new_s[:, :], start=True,
                                 stop=True)
            last.then_inc(S["new_spread"], 1)

        @block.scalar
        def _(act):
            for m in range(16 * PAIRS):
                act.wait_ge(S["turned"], m + 1)
                if m >= 2:
                    act.wait_ge(S["scored"], m - 1)
                act.activation(kT[m % 2][:, :], ps_t[m % 2][:, :], ACT.Copy).then_inc(S["turn_copied"], 1)

        @block.vector
        def _(dve):
            link = Chain(dve, S["step"])
            qi = keep["small"][0:NB, F_QI:F_QKV]
            for i in range(2):
                dve.tensor_copy(qi2[:, :, i, :], qi.rearrange("b (h e) -> b h e", h=IDX_HEADS)).then_inc(S["q_twice"], 1)
            dve.memset(q_blk[:, :, :, :], 0.0).then_inc(S["q_block_ready"], 1)
            dve.wait_ge(S["q_block_ready"], 1)
            dve.wait_ge(S["q_turned"], 1)
            for i in range(2):
                dve.tensor_copy(q_blk[64 * i:64 * i + 64, :, i, :], ps_q[64 * i:64 * i + 64, 0:P].rearrange(
                    "p (h b) -> p b h", b=NB)).then_inc(S["q_block_ready"], 1)
            ki = keep["samp"][:, T_KI:T_KI + DH].unsqueeze(1).broadcast_to([NB, IDX_HEADS, DH])
            link(dve.tensor_tensor(new[:, :, :], qi.rearrange("b (h e) -> b h e", h=IDX_HEADS), ki, ALU.mult))
            link(dve.tensor_reduce(new_h[:, :], new[:, :, :], AX.X, ALU.add))
            link(dve.scalar_tensor_tensor(out=new_h[:, :], in0=new_h[:, :], scalar=0.0,
                                          in1=keep["samp"][:, T_WI:T_WI + IDX_HEADS], op0=ALU.max, op1=ALU.mult))
            dve.tensor_reduce(new_s[:, :], new_h[:, :], AX.X, ALU.add).then_inc(S["new_ready"], 1)
            for n in range(PAIRS):
                dve.wait_ge(S["w_ready"], n + 1)
                dve.tensor_copy(w_row[:, :], ps_w[:, 0:IDX_HEADS]).then_inc(S["w_copied"], 1)
                dve.wait_ge(S["w_copied"], n + 1)
                for b in range(2):
                    dve.wait_ge(S["scored"], 16 * n + 8 * b + 8)
                    dve.scalar_tensor_tensor(out=prod[:, :, :], in0=ps_s[b][:, :].rearrange(
                        "p (c h) -> p c h", h=IDX_HEADS), scalar=0.0,
                        in1=w_row[:, :].unsqueeze(1).broadcast_to([P, 64, IDX_HEADS]), op0=ALU.max,
                        op1=ALU.mult).then_inc(S["weighted"], 1)
                    dve.wait_ge(S["weighted"], 2 * n + b + 1)
                    link(dve.tensor_reduce(T["score"][:, n, 64 * b:64 * b + 64], prod[:, :, :], AX.X, ALU.add))
            dve.wait_ge(S["new_spread"], 1)
            link(dve.tensor_tensor(T["score"][:, :, PAGE:COLS], ps_q[:, 256:256 + PAIRS].unsqueeze(2),
                                   T["new_mask"][:, :].unsqueeze(1).broadcast_to([P, PAIRS, 1]), ALU.add))


def decode_select(nc, d, keep, T):
    with ExitStack() as ctx:
        s = Scope(nc, ctx)
        S = Sems(s, "ds_")
        PC = [P, PAIRS, COLS]
        hit = s.sb("s_hit", PC)
        sure = s.sb("s_sure", PC)
        edge = s.sb("s_edge", PC)
        rank = s.sb("s_rank", PC)
        rank_i = s.sb("s_rank_i", PC, I32)
        hi_i = s.sb("s_hi_i", PC, I32)
        hi_f = s.sb("s_hi_f", PC)
        lo_f = s.sb("s_lo_f", PC)
        mids = s.sb("s_mids", [P, BISECT + 1, PAIRS])
        pred = s.sb("s_pred", [P, BISECT, PAIRS])
        tmp = s.sb("s_tmp", [P, BISECT, PAIRS])
        delta = s.sb("s_delta", [P, BISECT + 1, PAIRS])
        bound = s.sb("s_bound", [P, 6, PAIRS])
        mrow = s.sb("s_mrow", [PAIRS, 2])
        mbc = s.sb("s_mbc", [PAIRS, 2, N_PAGES])
        hot_a = [s.sb(f"s_hot_a{i}", [P, COLS, 32]) for i in range(2)]
        hot_b = [s.sb(f"s_hot_b{i}", [P, COLS, 2, 16]) for i in range(2)]
        row_v = s.sb("s_row_value", PC)
        dist_v = s.sb("s_dist_value", [P, COLS])
        base = s.sb("s_page_base", [P, PAIRS])
        pg = s.sb("s_pages", [P, PAIRS], I32)
        i32f = s.sb("s_iota32", [P, 32])
        i32i = s.sb("s_iota32_i", [P, 32], I32)
        idx_f = s.sb("s_idx_i", [32, PAIRS, 32], I32)
        ps_c = s.ps("ps_cnt", [P, 512])
        ps_m = s.ps("ps_m", [P, 512])
        ps_x = [s.ps(f"ps_x{i}", [32, 512]) for i in range(2)]
        block = ctx.enter_context(nc.Block())

        def across(ap):
            return ap.unsqueeze(2).broadcast_to(PC)

        @block.sync
        def _(sp):
            for n in range(PAIRS):
                sp.dma_start(pg[:, n:n + 1], d["page_table"][2 * n:2 * n + 2, :].rearrange(
                    "s (g o) -> (s g) o", o=1)).then_inc(S["pages_loaded"], 16)
            sp.wait_ge(S["lists_ready"], PAIRS)
            for v in range(2):
                sp.dma_start(d["row_lists"][v].rearrange("(n a b) -> a n b", n=PAIRS, a=32),
                             idx_f[:, :, 16 * v:16 * v + 16]).then_inc(S["lists_stored"], 16)
            sp.wait_ge(S["lists_stored"], 32)
            for v in range(2):
                sp.dma_start(T["rows"][:, v, :], d["row_lists"][v].rearrange("(c p) -> p c", p=P)).then_inc(
                    S["lists_loaded"], 16)

        @block.gpsimd
        def _(pool):
            pool.iota(i32i[:, :], pattern=[[1, 32]], base=0, channel_multiplier=0).then_inc(S["iota"], 1)
            pool.wait_ge(S["iota"], 1)
            pool.tensor_copy(i32f[:, :], i32i[:, :]).then_inc(S["iota"], 1)
            pool.wait_ge(S["lists_loaded"], 32)
            for c in range(2 * NB):
                for src, dst, v in ((d["cache_k"], T["kg"][:, c, :], 0), (d["cache_v"], T["vg"][:, c, :], 0),
                                    (d["bias_rows"], T["bg"][:, c, :], 1)):
                    pool.indirect_dma_start(dst, None, src, bass.IndirectOffsetOnAxis(
                        ap=T["rows"][:, v, c:c + 1].bitcast(U32), axis=0)).then_inc(S["gathered"], 16)
            pool.wait_ge(S["gathered"], 16 * 6 * NB)

        @block.tensor
        def _(pe):
            pe.wait_ge(S["absmax"], 1)
            pe.transpose(ps_m[0:PAIRS, 0:P], bound[:, 0, :], keep["ident"][:, :]).then_inc(S["absmax_turned"], 1)
            pe.wait_ge(S["absmax_rows"], 1)
            pe.matmul(ps_m[:, P:P + PAIRS], mbc[:, :, :], keep["ident"][0:PAIRS, 0:PAIRS], start=True,
                      stop=True).then_inc(S["absmax_spread"], 1)
            for k in range(BISECT + 1):
                pe.wait_ge(S["counted"], k + 1)
                pe.matmul(ps_c[:, 0:PAIRS], T["same_half"][:, :, :], bound[:, 1, :], start=True,
                          stop=True).then_inc(S["summed"], 1)
            for k in range(2):
                pe.wait_ge(S["ranked"], k + 1)
                pe.matmul(ps_m[:, 256 + k * PAIRS:256 + (k + 1) * PAIRS], T["before"][:, :], bound[:, 5, :], start=True,
                          stop=True).then_inc(S["offset"], 1)
            for n in range(PAIRS):
                pe.wait_ge(S["hot_ready"], n + 1)
                if n >= 2:
                    pe.wait_ge(S["lists_ready"], n - 1)
                for c in range(COLS):
                    last = pe.matmul(ps_x[n % 2][:, 0:32], hot_a[n % 2][:, c, :], hot_b[n % 2][:, c, :, :],
                                     start=(c == 0), stop=(c == COLS - 1))
                last.then_inc(S["listed"], 1)
            for k in range(2):
                last = pe.matmul(ps_m[:, 384 + k * PAIRS:384 + (k + 1) * PAIRS], T["last_page"][:, k, :],
                                 edge[:, :, PAGE], start=True, stop=True)
            last.then_inc(S["new_flag"], 1)

        @block.vector
        def _(dve):
            link = Chain(dve, S["step"])
            score = T["score"][:, :, :]
            link(dve.tensor_tensor(hit[:, :, PAGE:COLS], score[:, :, PAGE:COLS],
                                   T["new_mask"][:, :].unsqueeze(1).broadcast_to([P, PAIRS, 1]), ALU.subtract))
            link(dve.tensor_copy(hit[:, :, 0:PAGE], score[:, :, 0:PAGE]))
            dve.tensor_reduce(bound[:, 0, :], hit[:, :, :], AX.X, ALU.max, apply_absolute_value=True).then_inc(
                S["absmax"], 1)
            dve.wait_ge(S["absmax_turned"], 1)
            link(dve.tensor_reduce(mrow[:, :], ps_m[0:PAIRS, 0:P].rearrange("n (s p) -> n s p", s=2), AX.X, ALU.max))
            dve.tensor_copy(mbc[:, :, :], mrow[:, :].unsqueeze(2).broadcast_to([PAIRS, 2, N_PAGES])).then_inc(
                S["absmax_rows"], 1)
            dve.wait_ge(S["absmax_spread"], 1)
            link(dve.tensor_copy(delta[:, 0, :], ps_m[:, P:P + PAIRS]))
            link(dve.tensor_copy(bound[:, 0, :], delta[:, 0, :]))
            for k in range(BISECT):
                link(dve.tensor_scalar(delta[:, k + 1, :], delta[:, k, :], 0.5, None, ALU.mult))
            link(dve.memset(mids[:, 0, :], 0.0))
            for k in range(BISECT):
                link(dve.tensor_tensor(hit[:, :, :], score, across(mids[:, k, :]), ALU.is_ge))
                dve.tensor_reduce(bound[:, 1, :], hit[:, :, :], AX.X, ALU.add).then_inc(S["counted"], 1)
                dve.wait_ge(S["summed"], k + 1)
                link(dve.tensor_scalar(pred[:, k, :], ps_c[:, 0:PAIRS], float(TOPK), 0.5, ALU.is_ge, ALU.subtract))
                link(dve.tensor_tensor(tmp[:, 0, :], pred[:, k, :], delta[:, k, :], ALU.mult))
                link(dve.tensor_tensor(mids[:, k + 1, :], mids[:, k, :], tmp[:, 0, :], ALU.add))
            for sign, row, op in ((ALU.subtract, 2, ALU.max), (ALU.add, 3, ALU.min)):
                link(dve.tensor_scalar(tmp[:, :, :], pred[:, :, :], 0.5, -NEG, sign, ALU.mult))
                link(dve.tensor_tensor(tmp[:, :, :], tmp[:, :, :], mids[:, 0:BISECT, :], ALU.add))
                link(dve.tensor_reduce(bound[:, row, :], tmp[:, :, :].rearrange("p k n -> p n k"), AX.X, op))
                if op == ALU.max:
                    link(dve.tensor_scalar(bound[:, 4, :], bound[:, 0, :], -1.0, None, ALU.mult))
                    link(dve.tensor_tensor(bound[:, row, :], bound[:, row, :], bound[:, 4, :], op))
                else:
                    link(dve.tensor_tensor(bound[:, row, :], bound[:, row, :], bound[:, 0, :], op))
            link(dve.tensor_tensor(sure[:, :, :], score, across(bound[:, 3, :]), ALU.is_gt))
            dve.tensor_reduce(bound[:, 1, :], sure[:, :, :], AX.X, ALU.add).then_inc(S["counted"], 1)
            link(dve.tensor_tensor(edge[:, :, :], score, across(bound[:, 2, :]), ALU.is_ge))
            link(dve.tensor_tensor(edge[:, :, :], edge[:, :, :], sure[:, :, :], ALU.subtract))
            dve.wait_ge(S["summed"], BISECT + 1)
            link(dve.tensor_scalar(bound[:, 4, :], ps_c[:, 0:PAIRS], -1.0, float(TOPK), ALU.mult, ALU.add))

            def ranks(src, k):
                for n in range(PAIRS):
                    link(dve.tensor_tensor_scan(rank[:, n, :], src[:, n, :], src[:, n, :], 0.0, ALU.add, ALU.max))
                dve.tensor_copy(bound[:, 5, :], rank[:, :, PAGE]).then_inc(S["ranked"], 1)
                dve.wait_ge(S["offset"], k + 1)
                link(dve.tensor_tensor(rank[:, :, :], rank[:, :, :], across(ps_m[:, 256 + k * PAIRS:256 + (k + 1) * PAIRS]),
                                       ALU.add))

            ranks(edge, 0)
            link(dve.tensor_tensor(rank[:, :, :], rank[:, :, :], across(bound[:, 4, :]), ALU.is_le))
            link(dve.tensor_tensor(edge[:, :, :], edge[:, :, :], rank[:, :, :], ALU.mult))
            link(dve.tensor_tensor(edge[:, :, :], edge[:, :, :], sure[:, :, :], ALU.add))
            ranks(edge, 1)
            link(dve.tensor_scalar(rank[:, :, :], rank[:, :, :], T["half_base"][:, 0:1], None, ALU.add))
            link(dve.tensor_tensor(rank[:, :, :], rank[:, :, :], edge[:, :, :], ALU.mult))
            link(dve.tensor_scalar(rank[:, :, :], rank[:, :, :], -1.0, None, ALU.add))
            link(dve.tensor_copy(rank_i[:, :, :], rank[:, :, :]))
            link(dve.tensor_scalar(hi_i[:, :, :], rank_i[:, :, :], 4, None, ALU.arith_shift_right))
            link(dve.tensor_copy(hi_f[:, :, :], hi_i[:, :, :]))
            link(dve.tensor_scalar(hi_i[:, :, :], rank_i[:, :, :], 15, None, ALU.bitwise_and))
            link(dve.tensor_copy(lo_f[:, :, :], hi_i[:, :, :]))
            dve.wait_ge(S["pages_loaded"], 16 * PAIRS)
            link(dve.tensor_copy(base[:, :], pg[:, :]))
            link(dve.tensor_scalar(base[:, :], base[:, :], float(PAGE), None, ALU.mult))
            col = T["iota_c"][:, :].unsqueeze(1).broadcast_to(PC)
            link(dve.tensor_tensor(row_v[:, :, :], col, across(base[:, :]), ALU.add))
            link(dve.memset(row_v[:, :, PAGE:COLS], 0.0))
            link(dve.tensor_scalar(dist_v[:, :], T["iota_c"][:, :], T["page_rel"][:, 0:1], 0.0, ALU.add, ALU.max))
            dve.wait_ge(S["iota"], 2)
            for n in range(PAIRS):
                u = n % 2
                if n >= 2:
                    dve.wait_ge(S["listed"], n - 1)
                link(dve.tensor_tensor(hot_a[u][:, :, :], hi_f[:, n, :].unsqueeze(2).broadcast_to([P, COLS, 32]),
                                       i32f[:, :].unsqueeze(1).broadcast_to([P, COLS, 32]), ALU.is_equal))
                link(dve.tensor_tensor(hot_b[u][:, :, 1, :], lo_f[:, n, :].unsqueeze(2).broadcast_to([P, COLS, 16]),
                                       i32f[:, 0:16].unsqueeze(1).broadcast_to([P, COLS, 16]), ALU.is_equal))
                link(dve.tensor_tensor(hot_b[u][:, :, 0, :], hot_b[u][:, :, 1, :],
                                       row_v[:, n, :].unsqueeze(2).broadcast_to([P, COLS, 16]), ALU.mult))
                dve.tensor_tensor(hot_b[u][:, :, 1, :], hot_b[u][:, :, 1, :],
                                  dist_v[:, :].unsqueeze(2).broadcast_to([P, COLS, 16]), ALU.mult).then_inc(
                    S["hot_ready"], 1)
                if n:
                    dve.wait_ge(S["listed"], n)
                    dve.tensor_copy(idx_f[:, n - 1, :], ps_x[(n - 1) % 2][:, 0:32]).then_inc(S["lists_ready"], 1)
            dve.wait_ge(S["listed"], PAIRS)
            dve.tensor_copy(idx_f[:, PAIRS - 1, :], ps_x[(PAIRS - 1) % 2][:, 0:32]).then_inc(S["lists_ready"], 1)
            dve.wait_ge(S["new_flag"], 1)
            link(dve.tensor_copy(T["flag"][:, :].rearrange("p (n s) -> p s n", s=2),
                                 ps_m[:, 384:384 + NB].rearrange("p (s n) -> p s n", s=2)))


def decode_attention(nc, d, keep, T):
    with ExitStack() as ctx:
        s = Scope(nc, ctx)
        S = Sems(s, "da_")
        B2H = [P, NB, 2, HEADS]
        prod = [s.sb(f"a_prod{i}", [P, 2, HEADS, DH]) for i in range(2)]
        lg = s.sb("a_logit", B2H)
        skip = s.sb("a_skip", [P, 2 * NB])
        dist = s.sb("a_dist", [P, 2 * NB])
        allmax = s.sb("a_allmax", B2H)
        m = s.sb("a_max", [P, NB, HEADS])
        e_new = s.sb("a_new", [P, NB, HEADS])
        off = s.sb("a_off", [P, NB])
        den = s.sb("a_den", [P, NB, HEADS])
        oT = s.sb("a_oT", [P, NB, HEADS])
        new_p = s.sb("a_new_prod", [NB, HEADS, DH])
        new_l = s.sb("a_new_logit", [NB, HEADS])
        b0 = s.sb("a_new_bias", [NB, HEADS])
        diag = s.sb("a_new_diag", [NB, NB, HEADS])
        vT = s.sb("a_vT", [P, NB])
        att = s.sb("a_att", [NB, 512])
        ps_q = [s.ps(f"ps_aq{i}", [P, 512]) for i in range(2)]
        ps_n = s.ps("ps_an", [P, 512])
        ps_o = s.ps("ps_ao", [P, 512])
        ps_r = s.ps("ps_ar", [NB, 1024])
        block = ctx.enter_context(nc.Block())

        @block.sync
        def _(sp):
            sp.dma_start(b0[:, :], d["bias_rows"][2 * P - 1].unsqueeze(0).broadcast_to([NB, HEADS])).then_inc(
                S["bias_loaded"], 16)
            sp.wait_ge(S["att_ready"], 1)
            sp.dma_start(d["mix"][SEQ:SEQ + NB, 0:512], att[:, :]).then_inc(S["att_stored"], 16)
            sp.wait_ge(S["att_stored"], 16)

        @block.gpsimd
        def _(pool):
            pool.wait_ge(S["logits_ready"], 1)
            pool.partition_all_reduce(allmax[:, :, :, :].rearrange("p b c h -> p (b c h)"),
                                      lg[:, :, :, :].rearrange("p b c h -> p (b c h)"), P,
                                      bass.bass_isa.ReduceOp.max).then_inc(S["max_ready"], 1)

        @block.tensor
        def _(pe):
            for b in range(NB):
                if b >= 2:
                    pe.wait_ge(S["q_read"], b - 1)
                for half in range(2):
                    last = pe.matmul(ps_q[b % 2][64 * half:64 * half + 64, :], T["seq_of"][:, b, :],
                                     keep["small"][0:NB, F_Q:F_QI], start=True, stop=True)
                last.then_inc(S["q_spread"], 1)
            pe.wait_ge(S["diag_ready"], 1)
            pe.matmul(ps_n[:, 0:64], keep["ones"][0:NB, :], diag[:, :, :], start=True, stop=True).then_inc(
                S["new_spread"], 1)
            pe.matmul(ps_n[:, 64:64 + NB], keep["samp"][:, T_V:T_V + P], keep["ident"][0:NB, 0:NB], start=True,
                      stop=True).then_inc(S["v_turned"], 1)
            pe.wait_ge(S["p_ready"], 1)
            pe.matmul(ps_n[:, P:2 * P], keep["ones"][:, :], lg[:, :, :, :], start=True, stop=True).then_inc(
                S["sums"], 1)
            for b in range(NB):
                for c in range(2):
                    last = pe.matmul(ps_o[:, b * HEADS:(b + 1) * HEADS], T["vg"][:, 2 * b + c, :], lg[:, b, c, :],
                                     start=(c == 0), stop=(c == 1))
            last.then_inc(S["values"], 1)
            pe.wait_ge(S["out_ready"], 1)
            for h in range(HEADS):
                last = pe.matmul(ps_r[:, h * P:(h + 1) * P], oT[:, :, h], keep["ident"][:, :], start=True, stop=True)
            last.then_inc(S["out_turned"], 1)

        @block.scalar
        def _(act):
            act.wait_ge(S["shifted"], 2)
            act.activation(lg[:, :, :, :], lg[:, :, :, :], ACT.Exp).then_inc(S["p_ready"], 1)
            act.activation(e_new[:, :, :], e_new[:, :, :], ACT.Exp).then_inc(S["p_ready"], 1)

        @block.vector
        def _(dve):
            link = Chain(dve, S["step"])
            link(dve.tensor_copy(dist[:, :], T["rows"][:, 1, :]))
            link(dve.tensor_scalar(skip[:, :], dist[:, :], 2.0 * P - 1, NEG, ALU.is_equal, ALU.mult))
            for b in range(NB):
                dve.wait_ge(S["q_spread"], b + 1)
                for c in range(2):
                    ins = dve.tensor_tensor(
                        prod[b % 2][:, c, :, :].rearrange("p (g r) e -> p g r e", g=KV_HEADS),
                        T["kg"][:, 2 * b + c, :].rearrange("p (g e) -> p g e", g=KV_HEADS).unsqueeze(2).broadcast_to(
                            [P, KV_HEADS, 4, DH]),
                        ps_q[b % 2][:, :].rearrange("p (g r e) -> p g r e", g=KV_HEADS, r=4), ALU.mult)
                    if c == 0:
                        link(ins)
                    else:
                        ins.then_inc(S["q_read"], 1)
                dve.wait_ge(S["q_read"], b + 1)
                link(dve.tensor_reduce(lg[:, b, :, :], prod[b % 2][:, :, :, :], AX.X, ALU.add))
            lgf = lg[:, :, :, :].rearrange("p b c h -> p (b c) h")
            link(dve.scalar_tensor_tensor(out=lgf, in0=lgf, scalar=DH ** -0.5, in1=T["bg"][:, :, :], op0=ALU.mult,
                                          op1=ALU.add))
            dve.tensor_tensor(lgf, lgf, skip[:, :].unsqueeze(2).broadcast_to([P, 2 * NB, HEADS]), ALU.add).then_inc(
                S["logits_ready"], 1)
            link(dve.tensor_tensor(
                new_p[:, :, :].rearrange("p (g r) e -> p g r e", g=KV_HEADS),
                keep["small"][0:NB, F_Q:F_QI].rearrange("p (g r e) -> p g r e", g=KV_HEADS, r=4),
                keep["samp"][:, T_K:T_K + P].rearrange("p (g e) -> p g e", g=KV_HEADS).unsqueeze(2).broadcast_to(
                    [NB, KV_HEADS, 4, DH]), ALU.mult))
            link(dve.tensor_reduce(new_l[:, :], new_p[:, :, :], AX.X, ALU.add))
            dve.wait_ge(S["bias_loaded"], 16)
            link(dve.scalar_tensor_tensor(out=new_l[:, :], in0=new_l[:, :], scalar=DH ** -0.5, in1=b0[:, :],
                                          op0=ALU.mult, op1=ALU.add))
            dve.tensor_tensor(diag[:, :, :], new_l[:, :].unsqueeze(1).broadcast_to([NB, NB, HEADS]),
                              keep["ident"][0:NB, 0:NB].unsqueeze(2).broadcast_to([NB, NB, HEADS]),
                              ALU.mult).then_inc(S["diag_ready"], 1)
            link(dve.tensor_scalar(off[:, :], T["flag"][:, :], 1.0, -NEG, ALU.subtract, ALU.mult))
            dve.wait_ge(S["new_spread"], 1)
            dve.wait_ge(S["v_turned"], 1)
            link(dve.tensor_tensor(e_new[:, :, :], ps_n[:, 0:64].rearrange("p (b h) -> p b h", h=HEADS),
                                   off[:, :].unsqueeze(2).broadcast_to([P, NB, HEADS]), ALU.add))
            dve.wait_ge(S["max_ready"], 1)
            link(dve.tensor_tensor(m[:, :, :], allmax[:, :, 0, :], allmax[:, :, 1, :], ALU.max))
            link(dve.tensor_tensor(m[:, :, :], m[:, :, :], e_new[:, :, :], ALU.max))
            dve.tensor_tensor(lg[:, :, :, :], lg[:, :, :, :], m[:, :, :].unsqueeze(2).broadcast_to(B2H),
                              ALU.subtract).then_inc(S["shifted"], 1)
            dve.tensor_tensor(e_new[:, :, :], e_new[:, :, :], m[:, :, :], ALU.subtract).then_inc(S["shifted"], 1)
            dve.wait_ge(S["sums"], 1)
            dve.wait_ge(S["p_ready"], 2)
            sums = ps_n[:, P:2 * P].rearrange("p (b c h) -> p b c h", b=NB, c=2)
            link(dve.tensor_tensor(den[:, :, :], sums[:, :, 0, :], e_new[:, :, :], ALU.add))
            link(dve.tensor_tensor(den[:, :, :], den[:, :, :], sums[:, :, 1, :], ALU.add))
            link(dve.reciprocal(m[:, :, :], den[:, :, :]))
            link(dve.tensor_copy(vT[:, :], ps_n[:, 64:64 + NB]))
            link(dve.tensor_tensor(oT[:, :, :], e_new[:, :, :], vT[:, :].unsqueeze(2).broadcast_to([P, NB, HEADS]),
                                   ALU.mult))
            dve.wait_ge(S["values"], 1)
            link(dve.tensor_tensor(oT[:, :, :], oT[:, :, :], ps_o[:, 0:64].rearrange("p (b h) -> p b h", h=HEADS),
                                   ALU.add))
            dve.tensor_tensor(oT[:, :, :], oT[:, :, :], m[:, :, :], ALU.mult).then_inc(S["out_ready"], 1)
            dve.wait_ge(S["out_turned"], 1)
            for g in range(KV_HEADS):
                out = att[:, :].rearrange("b (h e) -> b h e", h=HEADS)[:, 4 * g:4 * g + 4, :]
                ins = dve.tensor_tensor(
                    out, ps_r[:, :].rearrange("b (h e) -> b h e", h=HEADS)[:, 4 * g:4 * g + 4, DH * g:DH * g + DH],
                    keep["samp_gate"][:, 0:512].rearrange("b (h e) -> b h e", h=HEADS)[:, 4 * g:4 * g + 4, :],
                    ALU.mult)
                if g == 0:
                    link(ins)
            ins.then_inc(S["att_ready"], 1)


def decode_delta(nc, d, keep):
    with ExitStack() as ctx:
        s = Scope(nc, ctx)
        S = Sems(s, "dd_")
        NS = NB * G_HEADS
        F = 3 * G_HEADS * GD
        ext = s.sb("g_ext", [NB, LAST, F])
        cw = s.sb("g_conv_w", [NB, CONV_W, F])
        acc = s.sb("g_acc", [NB, F])
        t1 = s.sb("g_t1", [NB, F])
        nrm = s.sb("g_norm", [NB, 8])
        st = s.sb("g_state", [P, NS, GD])
        eg = s.sb("g_eg", [NB, G_HEADS])
        diag = s.sb("g_diag", [NB, 2, NB, G_HEADS])
        bc = s.sb("g_bc", [P, 2, NS])
        qkvT = s.sb("g_qkvT", [P, 3, NS])
        dT = s.sb("g_deltaT", [P, NS])
        rows = s.sb("g_rows", [NS, 2, GD])
        outer = s.sb("g_outer", [NS, NS, GD])
        oT = s.sb("g_oT", [P, NS])
        osq = s.sb("g_osq", [P, NS])
        orr = s.sb("g_or", [P, NS])
        gn = s.sb("g_gnorm", [NB, GD])
        out = s.sb("g_out", [NB, 512])
        ps_t = s.ps("ps_gt", [P, 512])
        ps_k = s.ps("ps_gk", [P, 512])
        ps_r = s.ps("ps_gr", [NS, 512])
        ps_o = [s.ps(f"ps_go{i}", [P, 512]) for i in range(2)]
        ps_y = s.ps("ps_gy", [NB, 512])
        block = ctx.enter_context(nc.Block())
        raw = keep["small"][0:NB, F_QKV:F_ALL]

        @block.sync
        def _(sp):
            sp.dma_start(st[:, :, :], d["state_ssm"].rearrange("n d e -> d n e")).then_inc(S["state_loaded"], 16)
            sp.dma_start(ext[:, :, :], d["state_conv"]).then_inc(S["conv_loaded"], 16)
            sp.dma_start(cw[:, :, :], d["conv_w"].unsqueeze(0).broadcast_to([NB, CONV_W, F])).then_inc(
                S["conv_loaded"], 16)
            sp.dma_start(gn[:, :], d["gdn_norm"].broadcast_to([NB, GD])).then_inc(S["norm_loaded"], 16)
            sp.dma_start(d["conv_prompt"], keep["small"][NB:NB + LAST, F_QKV:F_ALL]).then_inc(S["stored"], 16)
            sp.dma_start(d["conv_sample"][:, LAST - 1, :], raw).then_inc(S["stored"], 16)
            sp.wait_ge(S["conv_loaded"], 32)
            sp.dma_start(d["conv_sample"][:, 0:LAST - 1, :], ext[:, 1:LAST, :]).then_inc(S["stored"], 16)
            sp.wait_ge(S["updated"], NS)
            sp.dma_start(d["ssm_sample"].rearrange("n d e -> d n e"), st[:, :, :]).then_inc(S["stored"], 16)
            sp.wait_ge(S["out_ready"], 1)
            sp.dma_start(d["mix"][SEQ:SEQ + NB, 512:1024], out[:, :]).then_inc(S["stored"], 16)
            sp.wait_ge(S["stored"], 80)

        @block.gpsimd
        def _(pool):
            pool.wait_ge(S["qk_sum"], 1)
            pool.tensor_tensor(nrm[:, :], nrm[:, :], keep["minus_half"][0:NB, 0:8], ALU.pow).then_inc(S["qk_norm"], 1)
            pool.wait_ge(S["o_mean"], 1)
            pool.tensor_tensor(orr[:, :], orr[:, :], keep["minus_half"][:, 0:NS], ALU.pow).then_inc(S["o_norm"], 1)

        @block.scalar
        def _(act):
            act.activation(eg[:, :], keep["dtab"][0:NB, NT, 7, :], ACT.Exp).then_inc(S["eg_ready"], 1)
            act.wait_ge(S["conv_done"], 1)
            act.activation(acc[:, :], acc[:, :], ACT.Silu).then_inc(S["silu_done"], 1)

        @block.tensor
        def _(pe):
            pe.wait_ge(S["diag_ready"], 2)
            pe.matmul(ps_k[:, 0:2 * NS], keep["ones"][0:NB, :], diag[:, :, :, :], start=True, stop=True).then_inc(
                S["bc_spread"], 1)
            pe.wait_ge(S["normed"], 2)
            for j in range(3):
                for h in range(G_HEADS):
                    c = j * NS + h
                    last = pe.matmul(ps_t[:, c:c + NS - G_HEADS + 1:G_HEADS],
                                     acc[:, (j * G_HEADS + h) * GD:(j * G_HEADS + h + 1) * GD],
                                     keep["ident"][0:NB, 0:NB], start=True, stop=True)
            last.then_inc(S["qkv_turned"], 1)
            pe.wait_ge(S["qkv_copied"], 1)
            pe.wait_ge(S["state_loaded"], 16)
            for n in range(NS):
                last = pe.matmul(ps_k[:, 128 + n:129 + n], st[:, n, :], qkvT[:, 1, n:n + 1], start=True, stop=True)
            last.then_inc(S["kv_ready"], 1)
            pe.wait_ge(S["delta_ready"], 1)
            pe.transpose(ps_r[:, 0:P], qkvT[:, 1, :], keep["ident"][:, :])
            pe.transpose(ps_r[:, P:2 * P], dT[:, :], keep["ident"][:, :]).then_inc(S["rows_turned"], 1)
            pe.wait_ge(S["outer_ready"], 1)
            for n in range(NS // 4):
                if n >= 2:
                    pe.wait_ge(S["updated"], 4 * (n - 1))
                pe.matmul(ps_o[n % 2][:, :], rows[:, 0, :], outer[:, 4 * n:4 * n + 4, :], start=True,
                          stop=True).then_inc(S["outer_done"], 1)
            pe.wait_ge(S["updated"], NS)
            for n in range(NS):
                last = pe.matmul(ps_k[:, 256 + n:257 + n], st[:, n, :], qkvT[:, 0, n:n + 1], start=True, stop=True)
            last.then_inc(S["o_ready"], 1)
            pe.wait_ge(S["o_squared"], 1)
            pe.matmul(ps_t[:, 256:256 + NS], keep["ones"][:, :], osq[:, :], start=True, stop=True).then_inc(
                S["o_summed"], 1)
            pe.wait_ge(S["o_normed"], 1)
            for h in range(G_HEADS):
                last = pe.matmul(ps_y[:, h * GD:(h + 1) * GD], oT[:, h:NS:G_HEADS], keep["ident"][:, :], start=True,
                                 stop=True)
            last.then_inc(S["o_turned"], 1)

        @block.vector
        def _(dve):
            link = Chain(dve, S["step"])
            dve.wait_ge(S["eg_ready"], 1)
            eye = keep["ident"][0:NB, 0:NB].unsqueeze(2).broadcast_to([NB, NB, G_HEADS])
            for i, src in enumerate((eg[:, :], keep["dtab"][0:NB, NT, 0, :])):
                dve.tensor_tensor(diag[:, i, :, :], src.unsqueeze(1).broadcast_to([NB, NB, G_HEADS]), eye,
                                  ALU.mult).then_inc(S["diag_ready"], 1)
            dve.wait_ge(S["conv_loaded"], 32)
            link(dve.tensor_tensor(acc[:, :], ext[:, 0, :], cw[:, 0, :], ALU.mult))
            for j in range(1, CONV_W):
                src = ext[:, j, :] if j < LAST else raw
                link(dve.tensor_tensor(t1[:, :], src, cw[:, j, :], ALU.mult))
                ins = dve.tensor_tensor(acc[:, :], acc[:, :], t1[:, :], ALU.add)
                if j < LAST:
                    link(ins)
            ins.then_inc(S["conv_done"], 1)
            dve.wait_ge(S["silu_done"], 1)
            qk = acc[:, 0:1024].rearrange("b (n e) -> b n e", n=8)
            link(dve.tensor_tensor(t1[:, 0:1024], acc[:, 0:1024], acc[:, 0:1024], ALU.mult))
            link(dve.tensor_reduce(nrm[:, :], t1[:, 0:1024].rearrange("b (n e) -> b n e", n=8), AX.X, ALU.add))
            dve.tensor_scalar(nrm[:, :], nrm[:, :], 1e-6, None, ALU.add).then_inc(S["qk_sum"], 1)
            dve.wait_ge(S["qk_norm"], 1)
            link(dve.tensor_scalar(nrm[:, 0:4], nrm[:, 0:4], GD ** -0.5, None, ALU.mult))
            dve.tensor_tensor(qk, qk, nrm[:, :].unsqueeze(2).broadcast_to([NB, 8, GD]), ALU.mult).then_inc(
                S["normed"], 2)
            dve.wait_ge(S["bc_spread"], 1)
            link(dve.tensor_copy(bc[:, :, :], ps_k[:, 0:2 * NS].rearrange("p (i n) -> p i n", i=2)))
            dve.wait_ge(S["qkv_turned"], 1)
            dve.tensor_copy(qkvT[:, :, :], ps_t[:, 0:3 * NS].rearrange("p (j n) -> p j n", j=3)).then_inc(
                S["qkv_copied"], 1)
            dve.wait_ge(S["qkv_copied"], 1)
            dve.wait_ge(S["kv_ready"], 1)
            link(dve.tensor_tensor(dT[:, :], ps_k[:, 128:128 + NS], bc[:, 0, :], ALU.mult))
            link(dve.tensor_tensor(dT[:, :], qkvT[:, 2, :], dT[:, :], ALU.subtract))
            dve.tensor_tensor(dT[:, :], dT[:, :], bc[:, 1, :], ALU.mult).then_inc(S["delta_ready"], 1)
            dve.wait_ge(S["rows_turned"], 1)
            link(dve.tensor_copy(rows[:, :, :], ps_r[:, 0:2 * P].rearrange("n (i e) -> n i e", i=2)))
            dve.tensor_tensor(outer[:, :, :], rows[:, 1, :].unsqueeze(1).broadcast_to([NS, NS, GD]),
                              keep["ident"][0:NS, 0:NS].unsqueeze(2).broadcast_to([NS, NS, GD]), ALU.mult).then_inc(
                S["outer_ready"], 1)
            for n in range(NS):
                dve.wait_ge(S["outer_done"], n // 4 + 1)
                dve.scalar_tensor_tensor(out=st[:, n, :], in0=st[:, n, :], scalar=bc[:, 0, n:n + 1],
                                         in1=ps_o[n // 4 % 2][:, (n % 4) * GD:(n % 4 + 1) * GD], op0=ALU.mult,
                                         op1=ALU.add).then_inc(S["updated"], 1)
            dve.wait_ge(S["o_ready"], 1)
            link(dve.tensor_copy(oT[:, :], ps_k[:, 256:256 + NS]))
            dve.tensor_tensor(osq[:, :], oT[:, :], oT[:, :], ALU.mult).then_inc(S["o_squared"], 1)
            dve.wait_ge(S["o_summed"], 1)
            dve.tensor_scalar(orr[:, :], ps_t[:, 256:256 + NS], 1.0 / GD, EPS, ALU.mult, ALU.add).then_inc(
                S["o_mean"], 1)
            dve.wait_ge(S["o_norm"], 1)
            dve.tensor_tensor(oT[:, :], oT[:, :], orr[:, :], ALU.mult).then_inc(S["o_normed"], 1)
            dve.wait_ge(S["o_turned"], 1)
            dve.wait_ge(S["norm_loaded"], 16)
            link(dve.tensor_tensor(out[:, :].rearrange("b (h e) -> b h e", h=G_HEADS),
                                   ps_y[:, :].rearrange("b (h e) -> b h e", h=G_HEADS),
                                   gn[:, :].unsqueeze(1).broadcast_to([NB, G_HEADS, GD]), ALU.mult))
            dve.tensor_tensor(out[:, :], out[:, :], keep["samp_gate"][:, 512:1024], ALU.mult).then_inc(
                S["out_ready"], 1)


def decode(nc, d, keep):
    with ExitStack() as ctx:
        s = Scope(nc, ctx)
        T = {"seq_of": s.sb("seq_of", [NB, NB, N_PAGES]), "last_page": s.sb("last_page", [P, 2, P]),
             "same_half": s.sb("same_half", [P, 2, N_PAGES]), "before": s.sb("before", [P, P]),
             "new_mask": s.sb("new_mask", [P, 1]), "half_base": s.sb("half_base", [P, 1]),
             "iota_i": s.sb("iota_i", [P, COLS], I32), "iota_c": s.sb("iota_c", [P, COLS]),
             "page_i": s.sb("page_i", [P, 1], I32), "page_f": s.sb("page_f", [P, 1]),
             "page_rel": s.sb("page_rel", [P, 1]),
             "score": s.sb("s_score", [P, PAIRS, COLS]), "rows": s.sb("s_rows", [P, 2, 2 * NB], I32),
             "flag": s.sb("s_flag", [P, NB]), "kg": s.sb("s_kg", [P, 2 * NB, P]),
             "vg": s.sb("s_vg", [P, 2 * NB, P]), "bg": s.sb("s_bg", [P, 2 * NB, HEADS])}
        decode_tables(nc, keep, T)
        decode_indexer(nc, d, keep, T)
        decode_select(nc, d, keep, T)
        decode_attention(nc, d, keep, T)
    decode_delta(nc, d, keep)


def build(nc, d):
    with ExitStack() as ctx:
        s = Scope(nc, ctx)
        keep = {
            "ident": s.sb("ident", [P, P]), "upper": s.sb("upper", [P, P]), "ones": s.sb("ones", [P, P]),
            "minus_half": s.sb("minus_half", [P, 64]),
            "tok": s.sb("tok", [P, NT, T_SMALL]), "samp": s.sb("samp", [NB, T_SMALL]),
            "samp_gate": s.sb("samp_gate", [NB, 1024]),
            "keyT": s.sb("keyT", [DH, KV_HEADS, SEQ]), "kidxT": s.sb("kidxT", [DH, SEQ]),
            "small": s.sb("small", [SMALL_ROWS, F_ALL]), "dtab": s.sb("dtab", [P, NT + 1, 8, G_HEADS]),
        }
        ctx.enter_context(nc.allow_non_contiguous_dma(reason="small tables by column"))
        constants(nc, keep)
        with ExitStack() as c2:
            s2 = Scope(nc, c2)
            hT = s2.sb("hT", [P, KB, SEQ])
            h_small = s2.sb("h_small", [P, KB, SMALL_ROWS])
            project_tokens(nc, d, keep, hT, h_small)
            transpose_keys(nc, keep)
            project_features(nc, d, keep, hT, h_small)
        decay_tables(nc, d, keep)
        delta_rule(nc, d, keep)
        keep["near"] = s.sb("near_bias", [P, HEADS, NEAR])
        bias_tables(nc, d, keep)
        decode(nc, d, keep)
        sparse_attention(nc, d, keep)
        output_projection(nc, d, keep)


_INS = ["x_prompt", "x_sample", "cache_k", "cache_v", "cache_kidx", "state_ssm", "state_conv", "page_table",
        "norm_in", "w_in", "conv_w", "a_log", "dt_bias", "gdn_norm", "w_out", "rel_table", "norm_final"]
_OUTS = [("y_prompt", (1, SEQ, D_MODEL), "b t d -> (b t) d"), ("y_sample", (NB, 1, D_MODEL), "b t d -> (b t) d"),
         ("k_prompt", (1, 1, SEQ, 2, 64), "l b t h d -> (l b t) (h d)"),
         ("v_prompt", (1, 1, SEQ, 2, 64), "l b t h d -> (l b t) (h d)"),
         ("kidx_prompt", (1, 1, SEQ, 64), "l b t d -> (l b t) d"),
         ("ssm_prompt", (1, 1, 4, 128, 128), "l b h d e -> (l b h) d e"),
         ("conv_prompt", (1, 1, 3, 1536), "l b t f -> (l b t) f"),
         ("k_sample", (1, NB, 1, 2, 64), "l b t h d -> (l b t) (h d)"),
         ("v_sample", (1, NB, 1, 2, 64), "l b t h d -> (l b t) (h d)"),
         ("kidx_sample", (1, NB, 1, 64), "l b t d -> (l b t) d"),
         ("ssm_sample", (1, NB, 4, 128, 128), "l b h d e -> (l b h) d e"),
         ("conv_sample", (1, NB, 3, 1536), "l b t f -> (l b) t f")]
_IN_VIEWS = {"x_prompt": "b t d -> (b t) d", "x_sample": "b t d -> (b t) d",
             "cache_k": "l n p h d -> (l n p) (h d)", "cache_v": "l n p h d -> (l n p) (h d)",
             "cache_kidx": "l n p d -> (l n p) d", "state_ssm": "l b h d e -> (l b h) d e",
             "state_conv": "l b t f -> (l b) t f", "norm_in": "l d -> (l d)", "w_in": "l d n -> (l d) n",
             "conv_w": "l j f -> (l j) f", "w_out": "l d n -> (l d) n"}


def kernel(**inputs):
    import numpy as _np
    import concourse.bacc as _bacc
    from concourse import mybir as _mybir
    from concourse.bass_utils import run_bass_kernel_spmd as _run

    nc = _bacc.Bacc("TRN2", target_bir_lowering=False, num_devices=1)
    arrays, d, nc_ap = {}, {}, {}
    for name in _INS:
        a = _np.ascontiguousarray(inputs[name])
        arrays[f"in_{name}"] = a
        ap = nc.dram_tensor(f"in_{name}", a.shape, _mybir.dt.from_np(a.dtype), kind="ExternalInput").ap()
        nc_ap[name] = ap
        d[name] = ap.rearrange(_IN_VIEWS[name]) if name in _IN_VIEWS else ap
    for name, shape, view in _OUTS:
        ap = nc.dram_tensor(f"out_{name}", shape, F32, kind="ExternalOutput").ap()
        d[name] = ap.rearrange(view)
    d["kidx_by_page"] = nc_ap["cache_kidx"].rearrange("l n p d -> (l n) (p d)")
    d["row_lists"] = nc.dram_tensor("row_lists", (2, NB * TOPK), I32).ap()
    d["gates"] = nc.dram_tensor("gates", (SEQ, 1024), F32).ap()
    d["featT"] = nc.dram_tensor("featT", (F_ALL, SEQ), F32).ap()
    d["mix"] = nc.dram_tensor("mix", (SEQ + NB, 1024), F32).ap()
    d["bias_vec"] = nc.dram_tensor("bias_vec", (HEADS, 3 * P), F32).ap()
    d["bias_rows"] = nc.dram_tensor("bias_rows", (3 * P, HEADS), F32).ap()
    hot = _np.zeros((N_BUCKETS, 3 * P), _np.float32)
    for m in range(3 * P):
        hot[max(b for b in range(N_BUCKETS) if BUCKET_START[b] <= max(2 * P - 1 - m, 0)), m] += 1
    hot[N_BUCKETS - 1] -= 1
    arrays["in_bucket_hot"] = hot
    d["bucket_hot"] = nc.dram_tensor("in_bucket_hot", hot.shape, F32, kind="ExternalInput").ap()
    build(nc, d)
    r = _run(nc, [arrays], core_ids=[0])
    return tuple(r.results[0][f"out_{name}"] for name, _, _ in _OUTS)
```
